# Optimizing a Trainium2 kernel written in Bass

```python
import jax, jax.numpy as jnp
from jax import lax
import numpy as np
import math

D_MODEL = 1024
BATCH = 1
SEQ = 512
DEPTH = 2

CHUNK = 64
N_MIXERS = 2
N_CONV_LAYERS = (DEPTH + 1) // 2
N_SSD_LAYERS = DEPTH // 2
N_MOD = 6
EPS = 1e-6

SC_WIDTH = 3

M_EXPAND = 2
M_D_INNER = M_EXPAND * D_MODEL
M_HEAD_DIM = 64
M_N_HEADS = M_D_INNER // M_HEAD_DIM
M_N_GROUPS = 8
M_HEADS_PER_GROUP = M_N_HEADS // M_N_GROUPS
M_D_STATE = 128
M_CONV_WIDTH = 4
M_CONV_DIM = M_D_INNER + 2 * M_N_GROUPS * M_D_STATE
M_IN_DIM = M_D_INNER + M_CONV_DIM + M_N_HEADS
SSD_CHUNK = CHUNK

D_FF = -(-8 * D_MODEL // (3 * 256)) * 256


def rms_normalize(x):
    xf = x.astype(jnp.float32)
    xf = xf * lax.rsqrt(jnp.mean(xf * xf, axis=-1, keepdims=True) + EPS)
    return xf.astype(x.dtype)

def rmsnorm(x, g):
    return rms_normalize(x) * g

def causal_depthwise_conv(x, w):
    k_width = w.shape[0]
    s = x.shape[1]
    xp = jnp.pad(x, ((0, 0), (k_width - 1, 0), (0, 0)))
    y = w[0] * xp[:, 0:s]
    for k in range(1, k_width):
        y = y + w[k] * xp[:, k:k + s]
    return y

def short_conv_mixer(h, w_in, conv_w, w_out):
    b_gate, c_gate, v = jnp.split(h @ w_in, 3, axis=-1)
    u = causal_depthwise_conv(c_gate * v, conv_w)
    return (b_gate * u) @ w_out

def ssd_chunked(xh, dt, a, bm, cm):
    bsz, s, g, r, p = xh.shape
    n = bm.shape[-1]
    nc, l = s // SSD_CHUNK, SSD_CHUNK
    dtype = xh.dtype
    xdt = (xh * dt[..., None].astype(dtype)).reshape(bsz, nc, l, g, r, p)
    bm = bm.reshape(bsz, nc, l, g, n)
    cm = cm.reshape(bsz, nc, l, g, n)
    cs = jnp.cumsum((dt * a).reshape(bsz, nc, l, g, r), axis=2)
    causal = jnp.tril(jnp.ones((l, l), dtype=bool))[None, None, :, :, None, None]
    seg = cs[:, :, :, None] - cs[:, :, None]
    decay = jnp.exp(jnp.where(causal, seg, -jnp.inf)).astype(dtype)
    cb = jnp.einsum('bclgn,bcsgn->bclsg', cm, bm)
    y_diag = jnp.einsum('bclsgr,bcsgrp->bclgrp', cb[..., None] * decay, xdt)
    decay_to_end = jnp.exp(cs[:, :, -1:] - cs).astype(dtype)
    states = jnp.einsum('bclgn,bclgr,bclgrp->bcgrpn', bm, decay_to_end, xdt)
    chunk_decay = jnp.exp(cs[:, :, -1]).astype(dtype)

    def step(state, inp):
        st, dec = inp
        return state * dec[..., None, None] + st, state

    h0 = jnp.zeros((bsz, g, r, p, n), dtype)
    _, prev = lax.scan(step, h0, (jnp.moveaxis(states, 1, 0), jnp.moveaxis(chunk_decay, 1, 0)))
    prev = jnp.moveaxis(prev, 0, 1)
    y_off = jnp.einsum('bclgn,bcgrpn,bclgr->bclgrp', cm, prev, jnp.exp(cs).astype(dtype))
    return (y_diag + y_off).reshape(bsz, s, g, r, p)

def ssd_mixer(h, w_in, conv_w, conv_b, dt_bias, a_log, d_skip, norm_g, w_out):
    bsz, s, _ = h.shape
    g, r, p, n = M_N_GROUPS, M_HEADS_PER_GROUP, M_HEAD_DIM, M_D_STATE
    z, xbc, dt_raw = jnp.split(h @ w_in, [M_D_INNER, M_D_INNER + M_CONV_DIM], axis=-1)
    xbc = jax.nn.silu(causal_depthwise_conv(xbc, conv_w) + conv_b)
    xs, bm, cm = jnp.split(xbc, [M_D_INNER, M_D_INNER + g * n], axis=-1)
    xs = xs.reshape(bsz, s, g, r, p)
    bm = bm.reshape(bsz, s, g, n)
    cm = cm.reshape(bsz, s, g, n)
    dt = jax.nn.softplus(dt_raw.astype(jnp.float32) + dt_bias.astype(jnp.float32)).reshape(bsz, s, g, r)
    a = -jnp.exp(a_log.astype(jnp.float32)).reshape(g, r)
    y = ssd_chunked(xs, dt, a, bm, cm) + d_skip.reshape(g, r)[:, :, None] * xs
    y = y.reshape(bsz, s, M_D_INNER) * jax.nn.silu(z)
    y = rms_normalize(y.reshape(bsz, s, g, M_D_INNER // g)).reshape(bsz, s, M_D_INNER) * norm_g
    return y @ w_out

def swiglu_ffn(h, w_in, w_out):
    gate, up = jnp.split(h @ w_in, 2, axis=-1)
    return (jax.nn.silu(gate) * up) @ w_out

def first_inputs(seed: int = 0) -> dict:
    key = jax.random.key(seed)
    ks = jax.random.split(key, 20)
    f32 = jnp.float32
    nrm = lambda k, shape, scale: jax.random.normal(k, shape, f32) * scale
    dt_init = jnp.exp(jax.random.uniform(ks[11], (N_SSD_LAYERS, M_N_HEADS), f32,
                                         np.log(1e-3), np.log(1e-1)))
    return {
        "x": nrm(ks[0], (BATCH, SEQ, D_MODEL), 1.0),
        "c": nrm(ks[1], (BATCH, D_MODEL), 1.0),
        "ada_w": nrm(ks[2], (D_MODEL, DEPTH * N_MOD * D_MODEL), 0.5 * D_MODEL ** -0.5),
        "ada_b": nrm(ks[3], (DEPTH * N_MOD * D_MODEL,), 0.02),
        "norm_g": 1.0 + nrm(ks[4], (DEPTH, 4, D_MODEL), 0.02),
        "a_w_in": nrm(ks[5], (N_CONV_LAYERS, D_MODEL, 3 * D_MODEL), D_MODEL ** -0.5),
        "a_conv_w": nrm(ks[6], (N_CONV_LAYERS, SC_WIDTH, D_MODEL), SC_WIDTH ** -0.5),
        "a_w_out": nrm(ks[7], (N_CONV_LAYERS, D_MODEL, D_MODEL), D_MODEL ** -0.5),
        "m_w_in": nrm(ks[8], (N_SSD_LAYERS, D_MODEL, M_IN_DIM), D_MODEL ** -0.5),
        "m_conv_w": nrm(ks[9], (N_SSD_LAYERS, M_CONV_WIDTH, M_CONV_DIM), M_CONV_WIDTH ** -0.5),
        "m_conv_b": nrm(ks[10], (N_SSD_LAYERS, M_CONV_DIM), 0.02),
        "m_dt_bias": dt_init + jnp.log(-jnp.expm1(-dt_init)),
        "m_a_log": jnp.log(jax.random.uniform(ks[12], (N_SSD_LAYERS, M_N_HEADS), f32, 1.0, 16.0)),
        "m_d": 1.0 + nrm(ks[13], (N_SSD_LAYERS, M_N_HEADS), 0.1),
        "m_norm_g": 1.0 + nrm(ks[14], (N_SSD_LAYERS, M_D_INNER), 0.02),
        "m_w_out": nrm(ks[15], (N_SSD_LAYERS, M_D_INNER, D_MODEL), M_D_INNER ** -0.5),
        "f_w_in": nrm(ks[16], (DEPTH, D_MODEL, 2 * D_FF), D_MODEL ** -0.5),
        "f_w_out": nrm(ks[17], (DEPTH, D_FF, D_MODEL), D_FF ** -0.5),
    }

def first_block(x, c, ada_w, ada_b, norm_g, a_w_in, a_conv_w, a_w_out, m_w_in, m_conv_w,
              m_conv_b, m_dt_bias, m_a_log, m_d, m_norm_g, m_w_out, f_w_in, f_w_out):
    bsz = x.shape[0]
    mod = (jax.nn.silu(c) @ ada_w + ada_b).reshape(bsz, DEPTH, 2, 3, D_MODEL)
    for i in range(DEPTH):
        j = i // N_MIXERS
        shift, scale, gate = (mod[:, i, 0, k][:, None, :] for k in range(3))
        h = rmsnorm(x, norm_g[i, 0]) * (1.0 + scale) + shift
        if i % N_MIXERS == 0:
            y = short_conv_mixer(h, a_w_in[j], a_conv_w[j], a_w_out[j])
        else:
            y = ssd_mixer(h, m_w_in[j], m_conv_w[j], m_conv_b[j], m_dt_bias[j], m_a_log[j],
                          m_d[j], m_norm_g[j], m_w_out[j])
        x = x + gate * rmsnorm(y, norm_g[i, 1])
        shift, scale, gate = (mod[:, i, 1, k][:, None, :] for k in range(3))
        h = rmsnorm(x, norm_g[i, 2]) * (1.0 + scale) + shift
        y = swiglu_ffn(h, f_w_in[i], f_w_out[i])
        x = x + gate * rmsnorm(y, norm_g[i, 3])
    return x


DEPTH_2 = 1

HEAD_DIM = 64
A_HEADS = 8
A_KV_HEADS = 2
A_WINDOW = 128
B_HEADS = 8
B_KV_GROUPS = 2
CMP_BLOCK = 32
CMP_STRIDE = 16
CMP_HIDDEN = 256
SLC_BLOCK = 64
SLC_TOPK = 16
NSA_WINDOW = 512
NUM_BUCKETS = 32
MAX_DISTANCE = 128
D_FF_2 = 2816
CONV_WIDTH = 3
Q_BLOCK = 128
NEG = -1e30
BIG = 1e30

A_Q_DIM = A_HEADS * HEAD_DIM
A_KV_DIM = A_KV_HEADS * HEAD_DIM
B_Q_DIM = B_HEADS * HEAD_DIM
B_KV_DIM = B_KV_GROUPS * HEAD_DIM
B_GATE_DIM = 3 * B_HEADS
IN_SPLITS = (A_Q_DIM, A_KV_DIM, A_KV_DIM, B_Q_DIM, B_KV_DIM, B_KV_DIM, B_KV_DIM, B_KV_DIM, B_KV_DIM, B_KV_DIM, B_GATE_DIM, D_MODEL, D_MODEL)
IN_DIM = sum(IN_SPLITS)
IN_OFFSETS = tuple(int(o) for o in np.cumsum(IN_SPLITS)[:-1])


def rmsnorm_2(x, g):
    xf = x.astype(jnp.float32)
    y = xf * lax.rsqrt(jnp.mean(xf * xf, axis=-1, keepdims=True) + EPS)
    return (y * g.astype(jnp.float32)).astype(x.dtype)

def t5_bucket(dist):
    dist = jnp.maximum(dist, 0)
    max_exact = NUM_BUCKETS // 2
    d = jnp.maximum(dist, 1).astype(jnp.float32)
    large = max_exact + (jnp.log(d / max_exact) / math.log(MAX_DISTANCE / max_exact)
                         * (NUM_BUCKETS - max_exact)).astype(jnp.int32)
    large = jnp.minimum(large, NUM_BUCKETS - 1)
    return jnp.where(dist < max_exact, dist, large)

def head_bias(table_gr, dist):
    return jnp.transpose(table_gr[t5_bucket(dist)], (2, 3, 0, 1))

def selection_overlap(n_cmp, n_slc):
    r = SLC_BLOCK // CMP_STRIDE
    c = CMP_BLOCK // CMP_STRIDE
    j, m, n = np.meshgrid(np.arange(n_slc), np.arange(r), np.arange(c), indexing='ij')
    i = r * j + m - n
    ok = (i >= 0) & (i < n_cmp)
    mat = np.zeros((n_cmp, n_slc), np.float32)
    np.add.at(mat, (i[ok], j[ok]), 1.0)
    return mat

def causal_dwconv(u, w, b):
    c = u.shape[-1]
    out = lax.conv_general_dilated(u, w[:, None, :].astype(u.dtype), window_strides=(1,),
                                   padding=[(CONV_WIDTH - 1, 0)],
                                   dimension_numbers=('NWC', 'WIO', 'NWC'),
                                   feature_group_count=c)
    return out + b

def swa_sink_attention(q, k, v, sinks, table):
    bsz, seq, n_heads, dh = q.shape
    n_groups = k.shape[2]
    rep = n_heads // n_groups
    span = A_WINDOW + Q_BLOCK
    qg = q.reshape(bsz, seq, n_groups, rep, dh)
    kp = jnp.pad(k, ((0, 0), (A_WINDOW, 0), (0, 0), (0, 0)))
    vp = jnp.pad(v, ((0, 0), (A_WINDOW, 0), (0, 0), (0, 0)))
    qi = jnp.arange(Q_BLOCK)[:, None]
    ki = jnp.arange(span)[None, :]
    dist = qi + A_WINDOW - ki
    in_window = (dist >= 0) & (dist < A_WINDOW)
    bias = head_bias(table.reshape(NUM_BUCKETS, n_groups, rep), dist)
    sink = sinks.astype(jnp.float32).reshape(n_groups, rep)
    scale = dh ** -0.5

    def block(b):
        start = b * Q_BLOCK
        qb = lax.dynamic_slice_in_dim(qg, start, Q_BLOCK, axis=1)
        kb = lax.dynamic_slice_in_dim(kp, start, span, axis=1)
        vb = lax.dynamic_slice_in_dim(vp, start, span, axis=1)
        valid = in_window & (start - A_WINDOW + ki >= 0)
        logits = jnp.einsum('bqgrd,bkgd->bgrqk', qb, kb, preferred_element_type=jnp.float32) * scale + bias
        logits = jnp.where(valid, logits, NEG)
        sink_col = jnp.broadcast_to(sink[None, :, :, None, None], logits.shape[:-1] + (1,))
        probs = jax.nn.softmax(jnp.concatenate([logits, sink_col], axis=-1), axis=-1)[..., :span]
        out = jnp.einsum('bgrqk,bkgd->bqgrd', probs.astype(v.dtype), vb)
        return out.reshape(bsz, Q_BLOCK, n_heads * dh)

    out = lax.map(block, jnp.arange(seq // Q_BLOCK))
    return jnp.transpose(out, (1, 0, 2, 3)).reshape(bsz, seq, n_heads * dh)

def compress(kv, pos, w1, w2):
    bsz, seq, n_groups, dh = kv.shape
    n_cmp = (seq - CMP_BLOCK) // CMP_STRIDE + 1
    idx = jnp.arange(n_cmp)[:, None] * CMP_STRIDE + jnp.arange(CMP_BLOCK)[None, :]
    blocks = kv[:, idx] + pos[None, None, :, None, :]
    blocks = jnp.transpose(blocks, (0, 1, 3, 2, 4)).reshape(bsz, n_cmp, n_groups, CMP_BLOCK * dh)
    return jax.nn.gelu(blocks @ w1) @ w2

def nsa_attention(q, k_cmp, v_cmp, k_slc, v_slc, k_win, v_win, gates, table):
    bsz, seq, n_heads, dh = q.shape
    n_groups = k_slc.shape[2]
    rep = n_heads // n_groups
    n_cmp = k_cmp.shape[1]
    n_slc = seq // SLC_BLOCK
    topk = min(SLC_TOPK, n_slc)
    n_tok = topk * SLC_BLOCK
    scale = dh ** -0.5
    qg = q.reshape(bsz, seq, n_groups, rep, dh)
    table_gr = table.reshape(NUM_BUCKETS, n_groups, rep)
    table_g = jnp.transpose(table_gr, (1, 0, 2))
    cmp_end = jnp.arange(n_cmp) * CMP_STRIDE + CMP_BLOCK - 1
    overlap = jnp.asarray(selection_overlap(n_cmp, n_slc))
    k_slc_g = jnp.transpose(k_slc, (0, 2, 1, 3))
    v_slc_g = jnp.transpose(v_slc, (0, 2, 1, 3))
    span = NSA_WINDOW + Q_BLOCK
    kwp = jnp.pad(k_win, ((0, 0), (NSA_WINDOW, 0), (0, 0), (0, 0)))
    vwp = jnp.pad(v_win, ((0, 0), (NSA_WINDOW, 0), (0, 0), (0, 0)))
    qi = jnp.arange(Q_BLOCK)[:, None]
    ki = jnp.arange(span)[None, :]
    dist_w = qi + NSA_WINDOW - ki
    in_window = (dist_w >= 0) & (dist_w < NSA_WINDOW)
    bias_w = head_bias(table_gr, dist_w)
    bidx = jnp.arange(bsz)[:, None, None, None]
    gidx = jnp.arange(n_groups)[None, :, None, None]
    slc_ids = jnp.arange(n_slc)[None, :]

    def block(b):
        start = b * Q_BLOCK
        qpos = start + jnp.arange(Q_BLOCK)
        qb = lax.dynamic_slice_in_dim(qg, start, Q_BLOCK, axis=1)
        dist_c = qpos[:, None] - cmp_end[None, :]
        valid_c = dist_c >= 0
        lc = jnp.einsum('bqgrd,bcgd->bgrqc', qb, k_cmp, preferred_element_type=jnp.float32) * scale
        lc = jnp.where(valid_c, lc + head_bias(table_gr, dist_c), NEG)
        p_c = jax.nn.softmax(lc, axis=-1) * valid_c
        o_c = jnp.einsum('bgrqc,bcgd->bqgrd', p_c.astype(v_cmp.dtype), v_cmp)
        imp = jnp.einsum('bgrqc,cj->bgqj', p_c, overlap)
        qblk = (qpos // SLC_BLOCK)[:, None]
        forced = (slc_ids == 0) | (slc_ids == qblk) | (slc_ids == qblk - 1)
        score = jnp.where(forced, BIG, jnp.where(slc_ids > qblk, NEG, imp))
        _, sel = lax.top_k(score, topk)
        tok = (sel[..., None] * SLC_BLOCK + jnp.arange(SLC_BLOCK)).reshape(bsz, n_groups, Q_BLOCK, n_tok)
        ks = k_slc_g[bidx, gidx, tok]
        vs = v_slc_g[bidx, gidx, tok]
        dist_s = qpos[None, None, :, None] - tok
        bias_s = jnp.transpose(table_g[gidx, t5_bucket(dist_s)], (0, 1, 4, 2, 3))
        ls = jnp.einsum('bqgrd,bgqtd->bgrqt', qb, ks, preferred_element_type=jnp.float32) * scale + bias_s
        ls = jnp.where((dist_s >= 0)[:, :, None], ls, NEG)
        p_s = jax.nn.softmax(ls, axis=-1)
        o_s = jnp.einsum('bgrqt,bgqtd->bqgrd', p_s.astype(v_slc.dtype), vs)
        kb = lax.dynamic_slice_in_dim(kwp, start, span, axis=1)
        vb = lax.dynamic_slice_in_dim(vwp, start, span, axis=1)
        valid_w = in_window & (start - NSA_WINDOW + ki >= 0)
        lw = jnp.einsum('bqgrd,bkgd->bgrqk', qb, kb, preferred_element_type=jnp.float32) * scale + bias_w
        p_w = jax.nn.softmax(jnp.where(valid_w, lw, NEG), axis=-1)
        o_w = jnp.einsum('bgrqk,bkgd->bqgrd', p_w.astype(v_win.dtype), vb)
        gb = lax.dynamic_slice_in_dim(gates, start, Q_BLOCK, axis=1)
        out = gb[..., 0:1] * o_c + gb[..., 1:2] * o_s + gb[..., 2:3] * o_w
        return out.reshape(bsz, Q_BLOCK, n_heads * dh)

    out = lax.map(block, jnp.arange(seq // Q_BLOCK))
    return jnp.transpose(out, (1, 0, 2, 3)).reshape(bsz, seq, n_heads * dh)

def second_inputs(seed: int = 0) -> dict:
    key = jax.random.key(seed)
    ks = jax.random.split(key, 20)
    f32 = jnp.float32

    def nrm(k, shape, scale):
        return jax.random.normal(k, shape, f32) * scale

    L, D = DEPTH_2, D_MODEL
    cmp_in = CMP_BLOCK * HEAD_DIM
    return {
        'x': nrm(ks[0], (BATCH, SEQ, D), 1.0),
        'norm_mix': 1.0 + nrm(ks[1], (L, D), 0.02),
        'w_in': nrm(ks[2], (L, D, IN_DIM), D ** -0.5),
        'attn_sinks': nrm(ks[3], (L, A_HEADS), 0.5),
        'cmp_pos_k': nrm(ks[4], (L, CMP_BLOCK, HEAD_DIM), 0.1),
        'cmp_w1_k': nrm(ks[5], (L, cmp_in, CMP_HIDDEN), cmp_in ** -0.5),
        'cmp_w2_k': nrm(ks[6], (L, CMP_HIDDEN, HEAD_DIM), CMP_HIDDEN ** -0.5),
        'cmp_pos_v': nrm(ks[7], (L, CMP_BLOCK, HEAD_DIM), 0.1),
        'cmp_w1_v': nrm(ks[8], (L, cmp_in, CMP_HIDDEN), cmp_in ** -0.5),
        'cmp_w2_v': nrm(ks[9], (L, CMP_HIDDEN, HEAD_DIM), CMP_HIDDEN ** -0.5),
        'w_up_a': nrm(ks[10], (L, A_Q_DIM, D), A_Q_DIM ** -0.5),
        'w_up_b': nrm(ks[11], (L, B_Q_DIM, D), B_Q_DIM ** -0.5),
        'w_out': nrm(ks[12], (L, D, D), D ** -0.5),
        'norm_ffn': 1.0 + nrm(ks[13], (L, D), 0.02),
        'w_ffn_in': nrm(ks[14], (L, D, 2 * D_FF_2), D ** -0.5),
        'conv_w': nrm(ks[15], (L, CONV_WIDTH, 2 * D_FF_2), CONV_WIDTH ** -0.5),
        'conv_b': nrm(ks[16], (L, 2 * D_FF_2), 0.01),
        'w_ffn_out': nrm(ks[17], (L, D_FF_2, D), D_FF_2 ** -0.5),
        'rel_bias_table': nrm(ks[18], (NUM_BUCKETS, A_HEADS + B_HEADS), 0.5),
        'norm_final': 1.0 + nrm(ks[19], (D,), 0.02),
    }

def second_block(x, norm_mix, w_in, attn_sinks, cmp_pos_k, cmp_w1_k, cmp_w2_k, cmp_pos_v, cmp_w1_v, cmp_w2_v,
              w_up_a, w_up_b, w_out, norm_ffn, w_ffn_in, conv_w, conv_b, w_ffn_out, rel_bias_table, norm_final):
    bsz, seq, _ = x.shape
    table_a = rel_bias_table[:, :A_HEADS]
    table_b = rel_bias_table[:, A_HEADS:]

    def heads(t, n):
        return t.reshape(bsz, seq, n, HEAD_DIM)

    for l in range(DEPTH_2):
        h = rmsnorm_2(x, norm_mix[l])
        proj = h @ w_in[l]
        (qa, ka, va, qb, kc, vc, ksl, vsl, kw, vw, g_nsa, g_a, g_b) = jnp.split(proj, IN_OFFSETS, axis=-1)
        y_a = swa_sink_attention(heads(qa, A_HEADS), heads(ka, A_KV_HEADS), heads(va, A_KV_HEADS),
                                 attn_sinks[l], table_a)
        k_cmp = compress(heads(kc, B_KV_GROUPS), cmp_pos_k[l], cmp_w1_k[l], cmp_w2_k[l])
        v_cmp = compress(heads(vc, B_KV_GROUPS), cmp_pos_v[l], cmp_w1_v[l], cmp_w2_v[l])
        nsa_gates = jax.nn.sigmoid(g_nsa).reshape(bsz, seq, B_KV_GROUPS, B_HEADS // B_KV_GROUPS, 3)
        y_b = nsa_attention(heads(qb, B_HEADS), k_cmp, v_cmp, heads(ksl, B_KV_GROUPS), heads(vsl, B_KV_GROUPS),
                            heads(kw, B_KV_GROUPS), heads(vw, B_KV_GROUPS), nsa_gates, table_b)
        merged = jax.nn.sigmoid(g_a) * (y_a @ w_up_a[l]) + jax.nn.sigmoid(g_b) * (y_b @ w_up_b[l])
        x = x + merged @ w_out[l]
        h = rmsnorm_2(x, norm_ffn[l])
        ug = causal_dwconv(h @ w_ffn_in[l], conv_w[l], conv_b[l])
        u, g = jnp.split(ug, 2, axis=-1)
        x = x + (jax.nn.silu(g) * u) @ w_ffn_out[l]
    return rmsnorm_2(x, norm_final)


def setup_inputs(seed=0):
    out = dict(first_inputs(seed))
    for name, value in second_inputs(seed + 1).items():
        if name != "x":
            out[name + "_2"] = value
    return out


def reference(
    x, c, ada_w, ada_b, norm_g, a_w_in, a_conv_w, a_w_out, m_w_in, m_conv_w, m_conv_b,
    m_dt_bias, m_a_log, m_d, m_norm_g, m_w_out, f_w_in, f_w_out, norm_mix_2, w_in_2,
    attn_sinks_2, cmp_pos_k_2, cmp_w1_k_2, cmp_w2_k_2, cmp_pos_v_2, cmp_w1_v_2, cmp_w2_v_2,
    w_up_a_2, w_up_b_2, w_out_2, norm_ffn_2, w_ffn_in_2, conv_w_2, conv_b_2, w_ffn_out_2,
    rel_bias_table_2, norm_final_2,
):
    x = first_block(
        x, c, ada_w, ada_b, norm_g, a_w_in, a_conv_w, a_w_out, m_w_in, m_conv_w, m_conv_b,
        m_dt_bias, m_a_log, m_d, m_norm_g, m_w_out, f_w_in, f_w_out,
    )
    return second_block(
        x, norm_mix_2, w_in_2, attn_sinks_2, cmp_pos_k_2, cmp_w1_k_2, cmp_w2_k_2, cmp_pos_v_2,
        cmp_w1_v_2, cmp_w2_v_2, w_up_a_2, w_up_b_2, w_out_2, norm_ffn_2, w_ffn_in_2, conv_w_2,
        conv_b_2, w_ffn_out_2, rel_bias_table_2, norm_final_2,
    )


_drawn_inputs = setup_inputs


def setup_inputs(seed=0):
    import zlib

    import numpy as np

    out = dict(_drawn_inputs(seed))
    spreads = {}
    factors = {'m_conv_b': 7.031,
     'm_d': 3.149,
     'm_norm_g': 8.0,
     'norm_mix_2': 8.0,
     'attn_sinks_2': 64.0,
     'cmp_pos_k_2': 8.0,
     'cmp_pos_v_2': 11.042,
     'norm_ffn_2': 4.268,
     'conv_b_2': 8.0}
    for name, (base, spread) in spreads.items():
        noise = np.random.default_rng([zlib.crc32(name.encode()), seed]).standard_normal(out[name].shape)
        drawn = base * np.exp(spread * noise) if base else spread * noise
        out[name] = __import__('jax').numpy.asarray(drawn.astype(out[name].dtype))
    for name, factor in factors.items():
        out[name] = (out[name] * factor).astype(out[name].dtype)
    return out
```

```python
from contextlib import ExitStack

import numpy as np

import concourse.bass as bass
from concourse import mybir

F32 = mybir.dt.float32
F32R = mybir.dt.float32r
ACT = mybir.ActivationFunctionType
ALU = mybir.AluOpType
AX = mybir.AxisListType

P = 128
S = 512
NT = S // P
D = 1024
KD = D // P
FF = 2816
KF = FF // P
EPS = 1e-6
RING = 4
CH = 8
NEG = -1e30

GROUPS = 8
HPG = 4
HEADS = GROUPS * HPG
GSTEP = 6
PACK = 1280
OFF_COL = {0: (512, 384), 2: (896, 128), 1: (1024, 256)}

CMP, STRIDE = 32, 16
NCMP = (S - CMP) // STRIDE + 1
WB = 1024
TB = 896
WA = 384
TA = 256
BUCKETS = 32

CHUNKS = dict(a_in=24, a_out=8, f_in0=44, f_out0=32, m_in=1 + GROUPS * GSTEP, m_out=16,
              f_in1=44, f_out1=32, w_in=33, cmp=8, up=8, w_out=8, g_in=44, g_out=32)
TILES = dict(a_in=24, a_out=8, f_in0=44, f_out0=8, m_in=1 + GROUPS * GSTEP, m_out=8,
             f_in1=44, f_out1=8, w_in=33, cmp=0, up=16, w_out=8, g_in=44, g_out=8)
INS = dict(a_in=8, a_out=8, f_in0=8, f_out0=22, m_in=8, m_out=16, f_in1=8, f_out1=22, w_in=8,
           cmp=0, up=8, w_out=8, g_in=8, g_out=22)


def starts(sizes):
    at, out = 0, {}
    for name, n in sizes.items():
        out[name] = at
        at += n
    return out, at


C0, NCH = starts(CHUNKS)
T0, _ = starts(TILES)
I0, _ = starts(INS)

VCOLS = dict(c=8, ada_b=96, norm_g=64, a_conv=24, m_conv=128, m_conv_b=32, m_norm=16, m_d=16,
             pos_k=16, pos_v=16, norm_mix=8, norm_ffn=8, norm_final=8, g_conv=132, g_conv_b=44)
V0, NV = starts(VCOLS)
KCOLS = dict(ident=128, tri=128, qvalid=4)
K0, NK = starts(KCOLS)


UNITS = [("C", e, 0) for e in range(2)] + [(k, e, q) for q in range(NT) for e in range(2) for k in "ASW"]


def span(kind, qt):
    return (max(0, (qt - 1) * P) if kind == "A" else 0), (qt + 1) * P


def program(nc, io):
    with ExitStack() as ctx:
        def sem(name):
            return ctx.enter_context(nc.semaphore(name))

        def sb(name, shape, dt=F32):
            return ctx.enter_context(nc.sbuf_tensor(name, shape, dt))

        raw = sb("raw", [P, RING, CH, P])
        whi = sb("whi", [P, RING, CH, P], F32R)
        wlo = sb("wlo", [P, RING, CH, P], F32R)
        x = sb("x", [P, KD, S])
        vec = sb("vec", [P, NV])
        kst = sb("kst", [P, NK])
        ones = sb("ones", [P, P])
        mod = sb("mod", [P, 96])
        csil = sb("csil", [P, KD])
        ncol = sb("ncol", [P, 4, 2, KD])
        zcol = sb("zcol", [P, 1])
        epscol = sb("epscol", [P, 1])
        dtp = sb("dtp", [HEADS, 4])
        acc = sb("acc", [P, S])
        sq = sb("sq", [P, 2, S])
        rstd = sb("rstd", [P, S])
        ta = sb("ta", [P, 2, S])
        tb = sb("tb", [P, 2, S])
        modacc = sb("modacc", [P, 2, 256])
        ident = kst[:, K0["ident"]:K0["ident"] + P]
        tri = kst[:, K0["tri"]:K0["tri"] + P]
        qvalid = kst[:, K0["qvalid"]:K0["qvalid"] + NT]

        def V(name, j):
            if isinstance(j, int):
                return vec[:, V0[name] + j:V0[name] + j + 1]
            return vec[:, bass.ds(V0[name] + j, 1)]

        def view(at, name, shape, dt=F32):
            with ExitStack() as v:
                if at:
                    v.enter_context(nc.sbuf_tensor(f"pad_{name}", [P, at // 4], F32))
                return v.enter_context(nc.sbuf_tensor(name, shape, dt))

        KB = 1024
        H = 0
        G = 32 * KB
        h_hi = view(H, "h_hi", [P, KD, S], F32R)
        h_lo = view(H + 16 * KB, "h_lo", [P, KD, S], F32R)
        g_hi = view(G, "g_hi", [P, KF, S], F32R)
        g_lo = view(G + 44 * KB, "g_lo", [P, KF, S], F32R)
        y = view(H, "y", [P, KD, S])
        ada_a = [view(at, f"ada_a{i}", [P, KD, 256]) for i, at in enumerate((G + 16 * KB, G + 24 * KB))]
        ada_f = [view(at, f"ada_f{i}", [P, KD, 256]) for i, at in enumerate((G + 36 * KB, G + 80 * KB))]
        y32 = view(G + 44 * KB, "y32", [P, 16, S])
        xg = view(G, "xg", [P, 2, 2, S])
        bg = view(G + 8 * KB, "bg", [P, 2, S])
        cg = view(G + 12 * KB, "cg", [P, 2, S])
        zg = view(G + 16 * KB, "zg", [P, 2, 2, S])
        csb = view(G + 24 * KB, "csb", [P, 2, PACK])
        eb = view(G + 34 * KB, "eb", [P, 2, PACK])
        cbm = view(G + 76 * KB, "cbm", [P, PACK])
        dt_tok = view(G + 81 * KB, "dt_tok", [P, NT, HEADS])
        cs_tok = view(G + 81 * KB + 512, "cs_tok", [P, NT, HEADS])
        ncs_tok = view(G + 81 * KB + 1024, "ncs_tok", [P, NT, HEADS])
        xdt = view(G + 83 * KB, "xdt", [P, NT, 2, P])
        dts = view(G + 24 * KB, "dts", [HEADS, 7, S])
        cs = view(G + 76 * KB, "cs", [HEADS, PACK])
        ga = view(G, "ga", [P, 16, S])
        qk = view(G + 32 * KB, "qk", [P, 13, S])
        vab = view(G + 58 * KB, "vab", [P, 3, NT, P])
        tbias = view(G + 64 * KB, "tbias", [P, 2, TB])
        abias = view(G + 71 * KB, "abias", [P, 2, TA])
        kc2 = view(G + 73 * KB, "kc2", [P, 2, 2, S])
        kcmp = view(G + 81 * KB, "kcmp", [P, 32])
        vcmp = view(G + 81 * KB + 128, "vcmp", [32, P])
        hid = view(G + 81 * KB + 640, "hid", [P, 2, 2, 64])
        qst = view(G + 83 * KB, "qst", [P, 2, S])
        gates = view(G + 87 * KB, "gates", [P, NT, 24])
        sinkb = view(G + 87 * KB + 384, "sinkb", [P, 8])
        stat = view(G + 87 * KB + 448, "stat", [P, 2, 8, NT])
        blk = view(H + 4 * KB, "blk", [P, 16, 2, NCMP])
        blk_hi = view(H + 8 * KB, "blk_hi", [P, 16, 2, NCMP], F32R)
        blk_lo = view(H + 12 * KB, "blk_lo", [P, 16, 2, NCMP], F32R)
        w2 = rstd[:, 0:256].rearrange("p (a m d) -> p a m d", a=2, m=2)
        hot = view(G + 62 * KB, "hot", [BUCKETS + 1, WB + WA])
        brow = view(G + 68 * KB, "brow", [16, WB + WA])
        tbl = view(G + 74 * KB, "tbl", [BUCKETS + 1, 16])
        mg_hi = view(G + 32 * KB, "mg_hi", [P, KD, S], F32R)
        mg_lo = view(G + 48 * KB, "mg_lo", [P, KD, S], F32R)

        psum = [ctx.enter_context(nc.psum_tensor(f"bank{b}", [P, S], F32)) for b in range(8)]

        raw_in = [sem(f"raw_in{s}") for s in range(RING)]
        hi_ready, lo_ready, chunk_done = sem("hi_ready"), sem("lo_ready"), sem("chunk_done")
        bank_free = [sem(f"bank_free{b}") for b in range(4)]
        in_hi, in_ready = sem("in_hi"), sem("in_ready")
        x_in, vec_in, const_ready, csil_ready, out_ready, out_done = (
            sem(n) for n in ("x_in", "vec_in", "const_ready", "csil_ready", "out_ready", "out_done"))
        ada_in = [sem("ada_in0"), sem("ada_in1")]
        mod_part, mod_sum, mod_out, ncol_ready = (sem(n) for n in ("mod_part", "mod_sum", "mod_out", "ncol_ready"))
        sq_out, acc_done, sum_done, std_out, x_done, t_out = (
            sem(n) for n in ("sq_out", "acc_done", "sum_done", "std_out", "x_done", "t_out"))
        dve_step = sem("dve_step")
        gate_out, prod_out = sem("gate_out"), sem("prod_out")
        dt_lin, dt_exp, a_exp, cs_ready, cs_out, tokT_done, tok_ready = (
            sem(n) for n in ("dt_lin", "dt_exp", "a_exp", "cs_ready", "cs_out", "tokT_done", "tok_ready"))
        grp_ready, xT_done, xdt_done, cb_done, cbm_dve, cbm_act = (
            sem(n) for n in ("grp_ready", "xT_done", "xdt_done", "cb_done", "cbm_dve", "cbm_act"))
        csb_in = [sem("csb_in0"), sem("csb_in1")]
        seg_done, exp_done, m_done, y_done, y_evac, yt_done, gsq_out, gacc, gsum, gstd, y32_out = (
            sem(n) for n in ("seg_done", "exp_done", "m_done", "y_done", "y_evac", "yt_done", "gsq_out", "gacc",
                             "gsum", "gstd", "y32_out"))
        tbl_in, hot_sum, brow_out, brow_wr, rows_wr, bias_in, sink_in, w2_in = (
            sem(n) for n in ("tbl_in", "hot_sum", "brow_out", "brow_wr", "rows_wr", "bias_in", "sink_in", "w2_in"))
        kc_in, blk_out, blk_split, blk_ready, hid_out, cmp_sum, cmp_out = (
            sem(n) for n in ("kc_in", "blk_out", "blk_split", "blk_ready", "hid_out", "cmp_sum", "cmp_out"))
        q_st, score_done, soft_done, pexp_done, pn_done, tr_done, pt_done, pv_done = (
            sem(n) for n in ("q_st", "score_done", "soft_done", "pexp_done", "pn_done", "tr_done", "pt_done", "pv_done"))

        block = ctx.enter_context(nc.Block())

        def tile(t, j):
            if isinstance(j, int):
                return t[:, j, :]
            return t[:, bass.ds(j, 1), :].rearrange("p a n -> p (a n)")

        def prob_buf(u):
            return (ta[:, 0, :], ta[:, 1, :], sq[:, 0, :])[u % 3]

        def turn(c, it, n):
            return c // RING + it * (n // RING)

        class Chain:

            def __init__(self, eng, steps):
                self.eng, self.steps, self.v, self.it, self.per = eng, steps, 0, 0, 0

            def loop(self, it, per):
                self.it, self.per, self.base = it, per, self.v

            def end(self, times):
                assert self.v - self.base == self.per, (self.v - self.base, self.per)
                self.v = self.base + times * self.per
                self.it = self.per = 0

            def __call__(self, ins):
                self.v += 1
                ins.then_inc(self.steps, 1)
                self.eng.wait_ge(self.steps, self.v + self.it * self.per)


        @block.sync
        def _(sp):
            def load(src, c, it=0, n=0, cols=CH * P):
                s = c % RING
                if c >= RING:
                    sp.wait_ge(lo_ready, c - RING + 1 + it * n)
                dst = raw[:, s].rearrange("p k m -> p (k m)")[:, 0:cols]
                sp.dma_start(dst, src).then_inc(raw_in[s], 16)

            def at(w, i):
                if isinstance(i, int):
                    return w[i]
                return w[bass.ds(i, 1)].rearrange("a p n -> (a p) n")

            def ada(ring, v, i):
                if not (isinstance(i, int) and i < 2):
                    sp.wait_ge(mod_part, i - 1)
                sp.dma_start(ring[v % 2].rearrange("p k n -> p (k n)"), at(io["ada"], i)).then_inc(ada_in[v % 2], 16)

            sp.dma_start(vec[:], io["vec"]).then_inc(vec_in, 16)
            sp.dma_start(x[:], io["x"].rearrange("p (k n) -> p k n", k=KD)).then_inc(x_in, 16)
            sp.dma_start(kst[:], io["kst"]).then_inc(vec_in, 16)
            sp.dma_start(dtp[:, 0:2], io["dtp"]).then_inc(vec_in, 16)
            sp.dma_start(tbl[:], io["tbl"]).then_inc(tbl_in, 16)
            sp.dma_start(hot[:], io["hot"]).then_inc(tbl_in, 16)
            for v in range(8):
                ada(ada_a, v, v)
                if v < 4:
                    load(io["a_in"][v], v)
            for j in range(8):
                for s in range(3):
                    c = 3 * j + s
                    if c >= 4:
                        load(io["a_in"][c], c)
                for u in range(2):
                    ada(ada_a, u, 8 + 2 * j + u)
                if j == 5:
                    sp.wait_ge(brow_out, 3)
                    sp.dma_start(io["brow"], brow[:]).then_inc(brow_wr, 16)
                if j >= 6:
                    sp.wait_ge(brow_wr, 16)
                    for hh in range(8 * (j - 6), 8 * (j - 5)):
                        n0, w = (0, WB) if hh >= 8 else (WB, WA)
                        dst = io["rows"][hh, 0:P * (w + 1)].rearrange("(p w) -> p w", p=P)[:, 0:w]
                        sp.dma_start(dst, io["brow"][hh:hh + 1, n0:n0 + w].broadcast_to([P, w])).then_inc(rows_wr, 16)

            def uniform(name):
                n = CHUNKS[name]
                with sp.Fori(0, n // RING) as it:
                    for u in range(RING):
                        load(at(io[name], it * RING + u), C0[name] + u, it, RING)
                for u in range(n - n % RING, n):
                    load(io[name][u], C0[name] + u)

            def pairs(name):
                with sp.Fori(0, 2) as it:
                    for m in range(4):
                        for u in range(4):
                            w = at(io[name], it * 8 + 2 * m + u // 2)
                            lo, hi = ((0, 6 * P), (6 * P, 11 * P))[u % 2]
                            load(w[:, lo:hi], C0[name] + 4 * m + u, it, 16, hi - lo)

            uniform("a_out")
            def chunks(it, n, first, last):
                for u in range(first, last):
                    load(at(io["f_in0"], it * n + u), C0["f_in0"] + u, it, n)

            def pair(v, it=0, n=0):
                for u in range(2):
                    ada(ada_f, v + u, it * n + (v + u))

            def turn_of(it, first, last):
                chunks(it, 8, first, first + 3)
                pair(26 + 6 * (first // 8 - 1), it, 6)
                chunks(it, 8, first + 3, first + 5)
                pair(28 + 6 * (first // 8 - 1), it, 6)
                chunks(it, 8, first + 5, first + 7)
                if not last:
                    pair(30 + 6 * (first // 8 - 1), it, 6)
                chunks(it, 8, first + 7, first + 8)

            chunks(0, 0, 0, 8)
            pair(24)
            with sp.Fori(0, 3) as it:
                turn_of(it, 8, False)
            turn_of(0, 32, True)
            chunks(0, 0, 40, CHUNKS["f_in0"])
            pairs("f_out0")

            def mixer_weights(i, it=0, n=0):
                load(at(io["m"], i + it * n), C0["m_in"] + i, it, n)

            def decay_row(r, h, first=False):
                if not first:
                    sp.wait_ge(exp_done, h - 1)
                src = io["cs"][h:h + 1, :] if isinstance(h, int) else io["cs"][bass.ds(h, 1), :]
                sp.dma_start(csb[:, r % 2, :], src.broadcast_to([P, PACK])).then_inc(csb_in[r % 2], 16)

            def body(G, it=0, n=0):
                c = 1 + GSTEP * (G + 1)
                h = HPG * (G - 1) + it * (HPG * n)
                mixer_weights(c + 1, it, GSTEP * n)
                for s in range(HPG):
                    mixer_weights(c + 2 + s, it, GSTEP * n)
                    decay_row(s, h + 2 + s)
                mixer_weights(c + GSTEP, it, GSTEP * n)

            for c in range(1 + GSTEP):
                mixer_weights(c)
            sp.wait_ge(cs_ready, 1)
            sp.dma_start(io["cs"], cs[:]).then_inc(cs_out, 16)
            for c in range(1 + GSTEP, 4 + GSTEP):
                mixer_weights(c)
            sp.wait_ge(cs_out, 16)
            sp.wait_ge(tok_ready, 3)
            for r in range(2):
                decay_row(r, r, True)
            for c in range(4 + GSTEP, 2 + 2 * GSTEP):
                mixer_weights(c)
            body(1)
            with sp.Fori(0, 3) as it:
                for b in range(2):
                    body(2 + b, it, 2)
            for r in range(2, HPG):
                decay_row(r, HPG * (GROUPS - 1) + r)
            for c in range(2 + GSTEP * (GROUPS + 1), CHUNKS["m_in"] + CHUNKS["m_out"]):
                mixer_weights(c)
            uniform("f_in1")
            pairs("f_out1")
            uniform("w_in")
            uniform("cmp")
            uniform("up")
            uniform("w_out")
            uniform("g_in")
            pairs("g_out")
            for k in range(KD):
                sp.wait_ge(out_ready, k + 1)
                sp.dma_start(io["out"][k], ta[:, k % 2, :]).then_inc(out_done, 16)
                sp.wait_ge(out_done, 16 * (k + 1))

        @block.gpsimd
        def _(pool):
            def split_lo(c, it=0):
                s = c % RING
                pool.wait_ge(hi_ready, c + 1 + it * RING)
                nc.gpsimd.tensor_tensor(wlo[:, s], raw[:, s], whi[:, s].bitcast(F32), ALU.subtract).then_inc(lo_ready, 1)

            with pool.Fori(0, NCH // RING) as it:
                for u in range(RING):
                    split_lo(u, it)
            for c in range(NCH - NCH % RING, NCH):
                split_lo(c)

        @block.tensor
        def _(pe):
            PRODUCTS = ((whi, "hi"), (whi, "lo"), (wlo, "hi"))

            def chunk(c, it, n, bank, ktiles, k0, xs, first, last, wait_in=None):
                s = c % RING
                pe.wait_ge(lo_ready, c + 1 + it * n)
                for kk in range(ktiles):
                    k = k0 + kk
                    if wait_in is not None:
                        pe.wait_ge(in_ready, wait_in + k + 1)
                    for i, (w, part) in enumerate(PRODUCTS):
                        mm = nc.tensor.matmul(psum[bank][:], w[:, s, kk, :], xs[part == "lo"][:, k, :],
                                              start=first and kk == 0 and i == 0,
                                              stop=last and kk == ktiles - 1 and i == 2)
                mm.then_inc(chunk_done, 1)

            def bank_of(t, it=0, n=0):
                b = t % 4
                if t >= 4:
                    pe.wait_ge(bank_free[b], t // 4 + it * (n // 4))
                return b

            def single(name, u, it=0, n=0, xs=(h_hi, h_lo), wait=True):
                b = bank_of(T0[name] + u, it, n)
                chunk(C0[name] + u, it, n, b, CH, 0, xs, True, True, I0[name] if wait else None)

            def down(name, it, xs):
                for m in range(4):
                    b = bank_of(T0[name] + m, it, 4)
                    k = 0
                    for u, n in enumerate((6, 5, 6, 5)):
                        chunk(C0[name] + 4 * m + u, it, 16, b, n, k, xs, u == 0, u == 3, I0[name] if m == 0 else None)
                        k += n

            def column_sums(n):
                pe.wait_ge(acc_done, KD * (n + 1))
                nc.tensor.matmul(psum[4][:], ones[:], acc[:], start=True, stop=True).then_inc(sum_done, 1)

            def modulation(v, i):
                pe.wait_ge(mod_part, i + 1)
                for b in range(2):
                    mm = nc.tensor.matmul(psum[5 + 2 * (v % 2)][:, b:b + 1], modacc[:, v % 2, b * P:(b + 1) * P],
                                          ones[:, 0:1], start=True, stop=True)
                mm.then_inc(mod_sum, 1)

            pe.wait_ge(const_ready, 1)
            column_sums(0)
            for v in range(8):
                modulation(v, v)
            for j in range(8):
                for s in range(3):
                    single("a_in", 3 * j + s)
                if j < 3:
                    if j == 0:
                        pe.wait_ge(tbl_in, 32)
                    else:
                        pe.wait_ge(brow_out, j)
                    e = min(S, WB + WA - S * j)
                    nc.tensor.matmul(psum[6][0:16, 0:e], tbl[:], hot[:, S * j:S * j + e], start=True, stop=True).then_inc(hot_sum, 1)
                for u in range(2):
                    modulation(u, 8 + 2 * j + u)
            with pe.Fori(0, 2) as it:
                for u in range(4):
                    single("a_out", u, it, 4, (g_hi, g_lo))
            column_sums(1)
            column_sums(2)

            def ffn(n):
                if n == 0:
                    with pe.Fori(0, 4) as it:
                        for u in range(8):
                            single("f_in0", u, it, 8, wait=u == 0)
                            if u in (3, 5, 7):
                                for v in range(24 + u - 3, 24 + u - 1):
                                    modulation(v, it * 6 + v)
                    with pe.Fori(0, 3) as it:
                        for u in range(4):
                            single("f_in0", 32 + u, it, 4, wait=False)
                else:
                    with pe.Fori(0, 11) as it:
                        for u in range(4):
                            single("f_in1", u, it, 4, wait=u == 0)
                with pe.Fori(0, 2) as it:
                    down(f"f_out{n}", it, (g_hi, g_lo))
                column_sums(3 + 4 * n)
                column_sums(4 + 4 * n)

            ffn(0)

            single("m_in", 0)
            pe.wait_ge(cs_ready, 1)
            for i in range(NT):
                nc.tensor.transpose(psum[4][:, i * HEADS:(i + 1) * HEADS], cs[:, i * P:(i + 1) * P], ident[0:HEADS, 0:HEADS])
                mm = nc.tensor.transpose(psum[5][:, i * HEADS:(i + 1) * HEADS], dts[:, 6, i * P:(i + 1) * P], ident[0:HEADS, 0:HEADS])
            mm.then_inc(tokT_done, 1)

            def ssd_sum(g):
                pe.wait_ge(gacc, g + 1)
                nc.tensor.matmul(psum[6][:], ones[:], sq[:, 0, :], start=True, stop=True).then_inc(gsum, 1)

            def ssd_turn(g, p):
                pe.wait_ge(grp_ready, 4 * (g + 1))
                for f in range(2):
                    for i in range(NT):
                        mm = nc.tensor.transpose(psum[4 + f][:, i * P:(i + 1) * P], xg[:, p, f, i * P:(i + 1) * P], ident)
                mm.then_inc(xT_done, 1)

            def ssd_cb(g, p):
                pe.wait_ge(xdt_done, 2 * (g + 1))
                for i in range(NT):
                    nc.tensor.matmul(psum[4][:, i * P:(i + 1) * P], bg[:, p, i * P:(i + 1) * P], cg[:, p, i * P:(i + 1) * P],
                                     start=True, stop=True)
                for i, b, col in ((0, 5, 0), (2, 5, 384), (1, 6, 0)):
                    n = OFF_COL[i][1]
                    mm = nc.tensor.matmul(psum[b][:, col:col + n], bg[:, p, i * P:(i + 1) * P], cg[:, p, (i + 1) * P:S],
                                          start=True, stop=True)
                mm.then_inc(cb_done, 1)

            def ssd_y(g, r, h):
                pe.wait_ge(m_done, h + 1)
                bank = psum[7 if r < 2 else 6]
                rows = slice(64 * (r % 2), 64 * (r % 2) + 64)
                for i in range(NT):
                    w = xdt[:, i, r // 2, 64 * (r % 2):64 * (r % 2) + 64]
                    mm = nc.tensor.matmul(bank[rows, i * P:(i + 1) * P], w, eb[:, r % 2, i * P:(i + 1) * P],
                                          start=i == 0, stop=i == NT - 1, skip_group_check=True)
                    if i in OFF_COL:
                        at, n = OFF_COL[i]
                        mm = nc.tensor.matmul(bank[rows, (i + 1) * P:S], w, eb[:, r % 2, at:at + n],
                                              start=False, stop=False, skip_group_check=True)
                mm.then_inc(y_done, 1)

            def m_body(G, it, n, g, gn, before, proj=True):
                def proj_chunk(s):
                    if proj:
                        single("m_in", 1 + GSTEP * G + s, it, n, wait=False)
                p = g % 2
                gi = g + it * gn
                hi = HPG * g + it * (gn * HPG)
                proj_chunk(0)
                if before:
                    ssd_sum(gi - 1)
                ssd_turn(gi, p)
                proj_chunk(1)
                if before:
                    pe.wait_ge(gstd, gi)
                ssd_cb(gi, p)
                for r in range(HPG):
                    proj_chunk(2 + r)
                    if r == 0 and before:
                        pe.wait_ge(y_evac, gi * 2)
                    if r == 2:
                        pe.wait_ge(cbm_act, (gi + 1) * 2)
                    ssd_y(gi, r, hi + r)

            for s in range(GSTEP):
                single("m_in", 1 + s, wait=False)
            pe.wait_ge(tok_ready, 3)
            m_body(1, 0, 0, 0, 0, False)
            with pe.Fori(0, 3) as it:
                for b in range(2):
                    m_body(2 + b, it, 2 * GSTEP, 1 + b, 2, True)
            m_body(8, 0, 0, 7, 0, True, proj=False)
            ssd_sum(7)
            with pe.Fori(0, 2) as it:
                for m in range(4):
                    b = bank_of(T0["m_out"] + m, it, 4)
                    for u in range(2):
                        chunk(C0["m_out"] + 2 * m + u, it, 8, b, CH, CH * u, (g_hi, g_lo), u == 0, u == 1, I0["m_out"])
            column_sums(5)
            column_sums(6)
            ffn(1)

            with pe.Fori(0, 3) as it:
                for u in range(4):
                    single("w_in", u, it, 4, wait=u == 0)
            for u in range(12, 29):
                single("w_in", u, wait=False)
            for u in range(4):
                c, n = C0["w_in"] + 29 + u, P if u < 3 else 24
                b = bank_of(T0["w_in"] + 29 + u)
                pe.wait_ge(lo_ready, c + 1)
                for i in range(NT):
                    for k in range(KD):
                        for j, (w, part) in enumerate(PRODUCTS):
                            mm = nc.tensor.matmul(psum[b][:, i * P:i * P + n],
                                                  (h_hi, h_lo)[part == "lo"][:, k, i * P:(i + 1) * P],
                                                  w[:, c % RING].rearrange("p k m -> p (k m)")[:, k * n:(k + 1) * n],
                                                  start=k == 0 and j == 0, stop=k == KD - 1 and j == 2)
                mm.then_inc(chunk_done, 1)

            for kv in range(2):
                pe.wait_ge(blk_ready, kv + 1)
                for m in range(2):
                    for half in range(2):
                        c = C0["cmp"] + 4 * kv + 2 * m + half
                        pe.wait_ge(lo_ready, c + 1)
                        for kk in range(CH):
                            for j, (w, part) in enumerate(PRODUCTS):
                                src = (blk_hi, blk_lo)[part == "lo"]
                                mm = nc.tensor.matmul(psum[4 + kv][:, m * 64:m * 64 + 2 * NCMP], w[:, c % RING, kk, :],
                                                      src[:, CH * half + kk].rearrange("p g c -> p (g c)"),
                                                      start=half == 0 and kk == 0 and j == 0, stop=half == 1 and kk == CH - 1 and j == 2)
                        mm.then_inc(chunk_done, 1)
            pe.wait_ge(w2_in, 32)
            pe.wait_ge(hid_out, 2)
            for e in range(2):
                for m in range(2):
                    nc.tensor.matmul(psum[6][64 * e:64 * e + 64, 0:NCMP], w2[:, 0, m, :], hid[:, 0, m, e * NCMP:(e + 1) * NCMP],
                                     start=m == 0, stop=m == 1)
            for e in range(2):
                for m in range(2):
                    mm = nc.tensor.matmul(psum[7][0:NCMP, 64 * e:64 * e + 64], hid[:, 1, m, e * NCMP:(e + 1) * NCMP], w2[:, 1, m, :],
                                          start=m == 0, stop=m == 1)
            mm.then_inc(cmp_sum, 1)

            pe.wait_ge(cmp_out, 2)
            for b in range(4):
                pe.wait_ge(bank_free[b], (T0["up"] - 1 - b) // 4 + 1)
            with pe.Fori(0, 4) as r:
                U = len(UNITS)

                def scores(u):
                    kind, e, qt = UNITS[u]
                    rows = slice(64 * e, 64 * e + 64)
                    bank = psum[u % 2]
                    if u == 0:
                        pe.wait_ge(q_st, 2 * r + 2)
                    if u >= 2:
                        pe.wait_ge(soft_done, r * U + u - 1)
                    if kind == "C":
                        for i in range(NT):
                            mm = nc.tensor.matmul(bank[:, i * 32:i * 32 + NCMP], qst[rows, 1, i * P:(i + 1) * P], kcmp[rows, 0:NCMP],
                                                  start=True, stop=True)
                    else:
                        k = qk[rows, 8 + "ASW".index(kind), :]
                        k0, k1 = span(kind, qt)
                        mm = nc.tensor.matmul(bank[:, 0:k1 - k0], qst[rows, int(kind != "A"), qt * P:(qt + 1) * P], k[:, k0:k1],
                                              start=True, stop=True)
                    mm.then_inc(score_done, 1)

                def turn_probs(u):
                    kind, e, qt = UNITS[u]
                    bank = psum[2 + u % 2]
                    pe.wait_ge(pn_done, r * U + u + 1)
                    if u >= 2:
                        pe.wait_ge(pt_done, r * U + u - 1)
                    sp_ = prob_buf(u)
                    if kind == "C":
                        for i in range(NT):
                            mm = nc.tensor.transpose(bank[0:NCMP, i * P:(i + 1) * P], sp_[:, i * 32:i * 32 + NCMP], ident)
                    else:
                        k0, k1 = span(kind, qt)
                        for i in range((k1 - k0) // P):
                            mm = nc.tensor.transpose(bank[:, i * P:(i + 1) * P], sp_[:, i * P:(i + 1) * P], ident)
                    mm.then_inc(tr_done, 1)

                def values(u):
                    kind, e, qt = UNITS[u]
                    rows = slice(64 * e, 64 * e + 64)
                    bank = psum[5 if kind == "A" else 6]
                    pe.wait_ge(pt_done, r * U + u + 1)
                    pt = tb[:, u % 2, :]
                    if kind == "C":
                        mm = nc.tensor.matmul(bank[rows, :], vcmp[0:NCMP, 64 * e:64 * e + 64], pt[0:NCMP, :],
                                              start=True, stop=False, skip_group_check=True)
                    else:
                        k0, k1 = span(kind, qt)
                        for i in range((k1 - k0) // P):
                            mm = nc.tensor.matmul(bank[rows, qt * P:(qt + 1) * P],
                                                  vab[:, "ASW".index(kind), k0 // P + i, 64 * e:64 * e + 64],
                                                  pt[:, i * P:(i + 1) * P], start=kind == "A" and i == 0, stop=False,
                                                  skip_group_check=True)
                    mm.then_inc(pv_done, 1)

                for u in range(2):
                    scores(u)
                for u in range(U):
                    if u + 2 < U:
                        scores(u + 2)
                    turn_probs(u)
                    if u >= 1:
                        values(u - 1)
                values(U - 1)

            for u in range(8):
                c = C0["up"] + u
                for half in range(2):
                    b = bank_of(T0["up"] + 2 * u + half)
                    if u == 0 and half == 0:
                        pe.wait_ge(lo_ready, c + 1)
                    elif half == 0:
                        pe.wait_ge(lo_ready, c + 1)
                    for kk in range(4):
                        k = 4 * half + kk
                        pe.wait_ge(in_ready, I0["up"] + 8)
                        for i, (w, part) in enumerate(PRODUCTS):
                            mm = nc.tensor.matmul(psum[b][:], w[:, c % RING, k, :], (h_hi, h_lo)[part == "lo"][:, k, :],
                                                  start=kk == 0 and i == 0, stop=kk == 3 and i == 2)
                mm.then_inc(chunk_done, 1)
            with pe.Fori(0, 2) as it:
                for u in range(4):
                    single("w_out", u, it, 4, (mg_hi, mg_lo))
            column_sums(9)
            with pe.Fori(0, 11) as it:
                for u in range(4):
                    single("g_in", u, it, 4, wait=u == 0)
            with pe.Fori(0, 2) as it:
                down("g_out", it, (g_hi, g_lo))
            column_sums(10)

        @block.scalar
        def _(act):
            def split_hi(c, it=0, n=0):
                if isinstance(it, int) and c + it * n >= NCH:
                    return
                s = c % RING
                act.wait_ge(raw_in[s], 16 * (turn(c, it, n) + 1))
                if c >= RING:
                    act.wait_ge(chunk_done, c - RING + 1 + it * n)
                nc.scalar.activation(whi[:, s], raw[:, s], ACT.Copy).then_inc(hi_ready, 1)

            def done(c, it=0, n=0):
                act.wait_ge(chunk_done, c + 1 + it * n)

            def read_out(t, it=0, n=0):
                act.wait_ge(bank_free[t % 4], t // 4 + 1 + it * (n // 4))

            def root(n):
                act.wait_ge(sum_done, n + 1)
                nc.scalar.activation(rstd[:], psum[4][:], ACT.Sqrt, bias=epscol[:], scale=1.0 / D).then_inc(std_out, 1)

            def square(src, n, k, it=0, per=0):
                if KD * n + k >= 2:
                    act.wait_ge(acc_done, KD * n + k - 1 + it * per)
                nc.scalar.activation(sq[:, k % 2, :], src, ACT.Square).then_inc(sq_out, 1)

            def x_squares(n, r):
                for k in range(KD):
                    act.wait_ge(x_done, KD * r + k + 1)
                    square(x[:, k, :], n, k)

            def norm_out(i, phase, a, b):
                for k in range(KD):
                    act.wait_ge(t_out, KD * i + k + 1)
                    if k >= 2:
                        act.wait_ge(in_ready, I0[phase] + k - 1)
                    nc.scalar.activation(tb[:, k % 2, :], ta[:, k % 2, :], ACT.Identity, bias=b(k), scale=a(k))
                    nc.scalar.activation(h_hi[:, k, :], ta[:, k % 2, :], ACT.Identity, bias=b(k), scale=a(k)).then_inc(in_hi, 1)

            def mod_norm(i, phase, q):
                norm_out(i, phase, lambda k: ncol[:, q, 0, k:k + 1], lambda k: mod[:, 3 * q * KD + k:3 * q * KD + k + 1])

            def plain_norm(i, phase, name):
                norm_out(i, phase, lambda k: V(name, k), lambda k: zcol[:])

            def y_tile(name, n, m, chunks, it=0):
                c = C0[name] + m * chunks
                for u in range(chunks - 1):
                    split_hi(c + RING + u, it, 4 * chunks)
                done(c + chunks - 1, it, 4 * chunks)
                b = (T0[name] + m) % 4
                square(psum[b][:], n, m, it, 4)
                nc.scalar.activation(tile(y, it * 4 + m), psum[b][:], ACT.Copy).then_inc(bank_free[b], 1)
                split_hi(c + RING + chunks - 1, it, 4 * chunks)

            act.wait_ge(vec_in, 48)
            nc.scalar.activation(csil[:], vec[:, V0["c"]:V0["c"] + KD], ACT.Silu).then_inc(csil_ready, 1)
            nc.scalar.activation(dtp[:, 2:3], dtp[:, 1:2], ACT.Exp).then_inc(a_exp, 1)
            act.wait_ge(x_in, 16)
            act.wait_ge(const_ready, 1)
            for k in range(KD):
                square(x[:, k, :], 0, k)
            root(0)
            for c in range(RING):
                split_hi(c)
            act.wait_ge(ncol_ready, 1)
            mod_norm(0, "a_in", 0)

            for j in range(8):
                c, t = C0["a_in"] + 3 * j, T0["a_in"] + 3 * j
                done(c)
                nc.scalar.activation(ta[:, j % 2, :], psum[t % 4][:], ACT.Copy).then_inc(bank_free[t % 4], 1)
                if 1 <= j <= 3:
                    act.wait_ge(hot_sum, j)
                    e = min(S * j, WB + WA)
                    nc.scalar.activation(brow[:, S * (j - 1):e], psum[6][0:16, 0:e - S * (j - 1)], ACT.Copy).then_inc(brow_out, 1)
                for u in range(3):
                    split_hi(c + RING + u)
                read_out(t + 2)
                nc.scalar.activation(g_hi[:, j, :], tb[:, j % 2, :], ACT.Copy).then_inc(in_hi, 1)
            with act.Fori(0, 2) as it:
                for m in range(4):
                    y_tile("a_out", 1, m, 1, it)
            root(1)
            x_squares(2, 0)
            root(2)
            act.wait_ge(ncol_ready, 2)
            mod_norm(1, "f_in0", 1)

            def ffn(n):
                f_in, f_out = f"f_in{n}", f"f_out{n}"
                with act.Fori(0, 11) as it:
                    for u in range(0, 4, 2):
                        c, t, j = C0[f_in] + u, T0[f_in] + u, u // 2
                        done(c, it, 4)
                        nc.scalar.activation(ta[:, j, :], psum[t % 4][:], ACT.Silu).then_inc(bank_free[t % 4], 1)
                        split_hi(c + RING, it, 4)
                        split_hi(c + RING + 1, it, 4)
                        read_out(t + 1, it, 4)
                        nc.scalar.activation(tile(g_hi, it * 2 + j), tb[:, j, :], ACT.Copy).then_inc(in_hi, 1)
                with act.Fori(0, 2) as it:
                    for m in range(4):
                        y_tile(f_out, 3 + 4 * n, m, 4, it)
                root(3 + 4 * n)
                x_squares(4 + 4 * n, 1 + 2 * n)
                root(4 + 4 * n)

            ffn(0)
            act.wait_ge(ncol_ready, 4)
            mod_norm(2, "m_in", 2)

            act.wait_ge(dt_lin, 1)
            nc.scalar.activation(dts[:, 1, :], dts[:, 0, :], ACT.Exp).then_inc(dt_exp, 1)
            split_hi(C0["m_in"] + RING)

            def conv_silu(G, s, it, n):
                t = T0["m_in"] + 1 + GSTEP * G + s
                read_out(t, it, n * GSTEP)
                dst = (xg[:, G % 2, 0], xg[:, G % 2, 1], bg[:, G % 2], cg[:, G % 2])[s]
                bias = V("m_conv_b", it * (4 * n) + 4 * G + s)
                if s == 0 and G >= 2:
                    act.wait_ge(yt_done, 2 * (G - 1) + it * (2 * n))
                nc.scalar.activation(dst, tb[:, s % 2, :], ACT.Silu, bias=bias).then_inc(grp_ready, 1)

            def evac(G, s, it, n):
                c, t = C0["m_in"] + 1 + GSTEP * G + s, T0["m_in"] + 1 + GSTEP * G + s
                if 1 <= s <= 4:
                    conv_silu(G, s - 1, it, n)
                if s >= 4:
                    done(c, it, n * GSTEP)
                    nc.scalar.activation(zg[:, G % 2, s - 4], psum[t % 4][:], ACT.Silu).then_inc(bank_free[t % 4], 1)
                split_hi(c + RING, it, n * GSTEP)

            def ssd_exp(h, r):
                act.wait_ge(csb_in[r % 2], 16 * (h // 2 + 1) if isinstance(h, int) else 16 * (h[0] // 2 + 1) + h[1] * (8 * h[2]))
                hv = h if isinstance(h, int) else h[0] + h[1] * h[2]
                if not (isinstance(h, int) and h < 2):
                    act.wait_ge(y_done, hv - 1)
                for i, (at, n) in OFF_COL.items():
                    bias = ncs_tok[:, i, hv:hv + 1] if isinstance(hv, int) else ncs_tok[:, i, bass.ds(hv, 1)]
                    nc.scalar.activation(eb[:, r % 2, at:at + n], csb[:, r % 2, at:at + n], ACT.Exp, bias=bias)
                act.wait_ge(seg_done, hv + 1)
                nc.scalar.activation(eb[:, r % 2, 0:S], eb[:, r % 2, 0:S], ACT.Exp).then_inc(exp_done, 1)

            def group_square(g, f):
                act.wait_ge(yt_done, g * 2 + f + 1)
                nc.scalar.activation(sq[:, f, :], ta[:, f, :], ACT.Square).then_inc(gsq_out, 1)

            def group_root(g):
                act.wait_ge(gsum, g + 1)
                nc.scalar.activation(rstd[:], psum[6][:], ACT.Sqrt, bias=epscol[:], scale=1.0 / 256).then_inc(gstd, 1)

            def m_body(G, it, n, g, before, proj=True):
                gi = g + it * n
                head = lambda r: HPG * g + r if isinstance(it, int) else (HPG * g + r, it, HPG * n)
                for s in range(GSTEP):
                    if s == 0 and before:
                        group_square(gi - 1, 1)
                    if s == 1:
                        if before:
                            group_root(gi - 1)
                        ssd_exp(head(0), 0)
                    if s == 2:
                        act.wait_ge(cb_done, gi + 1)
                        if before:
                            act.wait_ge(m_done, gi * HPG)
                        nc.scalar.activation(cbm[:, S:2 * S], psum[5][:], ACT.Copy).then_inc(cbm_act, 1)
                        nc.scalar.activation(cbm[:, 2 * S:PACK], psum[6][:, 0:PACK - 2 * S], ACT.Copy).then_inc(cbm_act, 1)
                    if 2 <= s <= 4:
                        ssd_exp(head(s - 1), s - 1)
                    if s == 4:
                        group_square(gi, 0)
                    if proj:
                        evac(G, s, it, n)

            for s in range(GSTEP):
                evac(0, s, 0, 0)
            act.wait_ge(tok_ready, 3)
            m_body(1, 0, 0, 0, False)
            with act.Fori(0, 3) as it:
                for b in range(2):
                    m_body(2 + b, it, 2, 1 + b, True)
            m_body(8, 0, 0, 7, True, proj=False)
            group_square(7, 1)
            group_root(7)
            act.wait_ge(y32_out, GROUPS)
            for k in range(16):
                nc.scalar.activation(g_hi[:, k, :], y32[:, k, :], ACT.Copy).then_inc(in_hi, 1)
            with act.Fori(0, 2) as it:
                for m in range(4):
                    y_tile("m_out", 5, m, 2, it)
            root(5)
            x_squares(6, 2)
            root(6)
            mod_norm(3, "f_in1", 3)
            ffn(1)
            plain_norm(4, "w_in", "norm_mix")

            with act.Fori(0, 3) as it:
                for u in range(4):
                    c, b = C0["w_in"] + u, (T0["w_in"] + u) % 4
                    done(c, it, 4)
                    nc.scalar.activation(tile(qk, it * 4 + u), psum[b][:], ACT.Copy).then_inc(bank_free[b], 1)
                    split_hi(c + RING, it, 4)
            act.dma_start(sinkb[:], io["sinks"].broadcast_to([P, 8])).then_inc(sink_in, 16)
            for u in range(12, 33):
                c, b = C0["w_in"] + u, (T0["w_in"] + u) % 4
                done(c)
                if u == 12:
                    nc.scalar.activation(qk[:, 12, :], psum[b][:], ACT.Copy).then_inc(bank_free[b], 1)
                elif u < 29:
                    nc.scalar.activation(ga[:, u - 13, :], psum[b][:], ACT.Sigmoid).then_inc(bank_free[b], 1)
                elif u < 32:
                    nc.scalar.activation(vab[:, u - 29].rearrange("p i n -> p (i n)"), psum[b][:], ACT.Copy).then_inc(bank_free[b], 1)
                else:
                    nc.scalar.activation(gates[:], psum[b][:].rearrange("p (i n) -> p i n", i=NT)[:, :, 0:24],
                                         ACT.Sigmoid).then_inc(bank_free[b], 1)
                split_hi(c + RING)
            for kv in range(2):
                act.dma_start(w2[:, kv], io["w2"][kv]).then_inc(w2_in, 16)

            for kv in range(2):
                b = (T0["w_in"] + 11 + kv) % 4
                act.wait_ge(bank_free[b], (T0["w_in"] + 11 + kv) // 4 + 1)
                for e in range(2):
                    src = qk[64 * e:64 * e + 64, 11 + kv, :]
                    act.dma_start(kc2[0:64, kv, e, :], src).then_inc(kc_in, 16)
                    act.dma_start(kc2[64:128, kv, e, 0:S - 1], src[:, 1:S]).then_inc(kc_in, 16)
            for kv in range(2):
                act.wait_ge(blk_out, kv + 1)
                if kv:
                    act.wait_ge(chunk_done, C0["cmp"] + 4)
                nc.scalar.activation(blk_hi[:], blk[:], ACT.Copy).then_inc(blk_split, 1)
                for u in range(4):
                    split_hi(C0["cmp"] + 4 * kv + u + RING)
                done(C0["cmp"] + 4 * kv + 3)
                nc.scalar.activation(hid[:, kv, :, 0:2 * NCMP],
                                     psum[4 + kv][:, 0:P].rearrange("p (m c) -> p m c", m=2)[:, :, 0:2 * NCMP],
                                     ACT.Gelu_apprx_tanh).then_inc(hid_out, 1)
            act.wait_ge(cmp_sum, 1)
            nc.scalar.activation(kcmp[:, 0:NCMP], psum[6][:, 0:NCMP], ACT.Copy).then_inc(cmp_out, 1)
            nc.scalar.activation(vcmp[0:NCMP, :], psum[7][0:NCMP, 0:P], ACT.Copy).then_inc(cmp_out, 1)

            act.wait_ge(sink_in, 16)
            act.wait_ge(rows_wr, 16 * 16)
            with act.Fori(0, 4) as r:
                U = len(UNITS)
                for e in range(2):
                    for first, w, n, dst in ((8, WB, TB, tbias), (0, WA, TA, abias)):
                        src = io["rows"][bass.ds(r + (first + 4 * e), 1), P - 1:P - 1 + P * w]
                        act.dma_start(dst[:, e, :], src.rearrange("a (p w) -> (a p) w", p=P)[:, 0:n]).then_inc(bias_in, 16)
                for i in range(2):
                    nc.scalar.activation(qst[:, i, :], tile(qk, r + 4 * i), ACT.Copy).then_inc(q_st, 1)

                def probs(u):
                    kind, e, qt = UNITS[u]
                    act.wait_ge(soft_done, r * U + u + 1)
                    st, p = stat[:, u % 2], prob_buf(u)
                    if kind == "C":
                        for i in range(NT):
                            last = nc.scalar.activation(p[:, i * 32:i * 32 + NCMP], p[:, i * 32:i * 32 + NCMP], ACT.Exp,
                                                        bias=st[:, 1, i:i + 1], accum_out=st[:, 2, i:i + 1])
                    else:
                        k0, k1 = span(kind, qt)
                        last = nc.scalar.activation(p[:, 0:k1 - k0], p[:, 0:k1 - k0], ACT.Exp, bias=st[:, 1, 0:1],
                                                    accum_out=st[:, 2, 0:1])
                    if kind == "A":
                        last = nc.scalar.activation(st[:, 3, 0:1], sinkb[:, bass.ds(r + 4 * e, 1)], ACT.Exp, bias=st[:, 1, 0:1])
                    last.then_inc(pexp_done, 1)

                def turned(u):
                    kind, e, qt = UNITS[u]
                    act.wait_ge(tr_done, r * U + u + 1)
                    if u >= 2:
                        act.wait_ge(pv_done, r * U + u - 1)
                    rows, n = (NCMP, S) if kind == "C" else (P, span(kind, qt)[1] - span(kind, qt)[0])
                    nc.scalar.activation(tb[0:rows, u % 2, 0:n], psum[2 + u % 2][0:rows, 0:n], ACT.Copy).then_inc(pt_done, 1)

                for u in range(U + 1):
                    if u < U:
                        probs(u)
                    if u >= 1:
                        turned(u - 1)
                act.wait_ge(pv_done, (r + 1) * U)
                for i in range(2):
                    nc.scalar.activation(ta[:, i, :], psum[5 + i][:], ACT.Copy)
                    nc.scalar.activation(tile(h_hi, r + 4 * i), psum[5 + i][:], ACT.Copy).then_inc(in_hi, 1)

            for u in range(8):
                act.wait_ge(prod_out, u + 1)
                nc.scalar.activation(mg_hi[:, u, :], ta[:, u % 2, :], ACT.Copy).then_inc(in_hi, 1)
                split_hi(C0["up"] + u + RING)
            with act.Fori(0, 2) as it:
                for u in range(4):
                    split_hi(C0["w_out"] + u + RING, it, 4)
                    read_out(T0["w_out"] + u, it, 4)
                    square(tile(x, it * 4 + u), 9, u, it, 4)
            root(9)
            plain_norm(5, "g_in", "norm_ffn")
            with act.Fori(0, 11) as it:
                for u in range(0, 4, 2):
                    c, t, j = C0["g_in"] + u, T0["g_in"] + u, u // 2
                    split_hi(c + RING, it, 4)
                    split_hi(c + RING + 1, it, 4)
                    read_out(t + 1, it, 4)
                    nc.scalar.activation(sq[:, j, :], tb[:, j, :], ACT.Silu, bias=V("g_conv_b", it * 2 + (KF + j))).then_inc(gate_out, 1)
                    act.wait_ge(prod_out, KD + it * 2 + (j + 1))
                    nc.scalar.activation(tile(g_hi, it * 2 + j), ta[:, j, :], ACT.Copy).then_inc(in_hi, 1)
            for m in range(8):
                for u in range(4):
                    split_hi(C0["g_out"] + 4 * m + u + RING)
                read_out(T0["g_out"] + m)
                square(x[:, m, :], 10, m)
            root(10)

        @block.vector
        def _(dve):
            TT, TS, STT = nc.vector.tensor_tensor, nc.vector.tensor_scalar, nc.vector.scalar_tensor_tensor
            step = Chain(dve, dve_step)

            def done(c, it=0, n=0):
                dve.wait_ge(chunk_done, c + 1 + it * n)

            def read_out(t, it=0, n=0):
                dve.wait_ge(bank_free[t % 4], t // 4 + 1 + it * (n // 4))

            def lo_part(dst, whole, hi, i):
                dve.wait_ge(in_hi, i + 1)
                TT(dst, whole, hi.bitcast(F32), ALU.subtract).then_inc(in_ready, 1)

            def clear_acc():
                step(nc.vector.memset(acc[:], 0.0))

            def add_square(n, k, it=0, per=0):
                dve.wait_ge(sq_out, KD * n + k + 1 + it * per)
                if KD * n + k:
                    dve.wait_ge(acc_done, KD * n + k + it * per)
                TT(acc[:], acc[:], sq[:, k % 2, :], ALU.add).then_inc(acc_done, 1)

            def reciprocal(n):
                dve.wait_ge(std_out, n + 1)
                step(nc.vector.reciprocal(rstd[:], rstd[:]))

            def residual(r, n):
                reciprocal(n - 1)
                clear_acc()
                for k in range(KD):
                    step(TT(ta[:, k % 2, :], y[:, k, :], rstd[:], ALU.mult))
                    STT(out=x[:, k, :], in0=ta[:, k % 2, :], scalar=ncol[:, r, 1, k:k + 1], in1=x[:, k, :],
                        op0=ALU.mult, op1=ALU.add).then_inc(x_done, 1)
                    if k >= 1:
                        add_square(n, k - 1)
                add_square(n, KD - 1)

            def norm_in(i, n, phase):
                reciprocal(n)
                for k in range(KD + 1):
                    if k < KD:
                        if k >= 2:
                            dve.wait_ge(in_hi, I0[phase] + k - 1)
                        TT(ta[:, k % 2, :], x[:, k, :], rstd[:], ALU.mult).then_inc(t_out, 1)
                    if k >= 1:
                        lo_part(h_lo[:, k - 1, :], tb[:, (k - 1) % 2, :], h_hi[:, k - 1, :], I0[phase] + k - 1)

            def mod_evac(v, it=0):
                i = v + it * 6
                dve.wait_ge(mod_sum, i + 1)
                dst, b = ((mod[:, 2 * v:2 * v + 2], vec[:, V0["ada_b"] + 2 * v:V0["ada_b"] + 2 * v + 2]) if isinstance(it, int)
                          else (mod[:, bass.ds(i * 2, 2)], vec[:, bass.ds(i * 2 + V0["ada_b"], 2)]))
                TT(dst, psum[5 + 2 * (v % 2)][:, 0:2], b, ALU.add).then_inc(mod_out, 1)

            def mod_unit(v, ring, it=0):
                if v >= 2:
                    mod_evac(v - 2, it)
                dve.wait_ge(ada_in[v % 2], 16 * (v // 2 + 1) + it * (16 * 3))
                out = modacc[:, v % 2, :]
                step(TS(out, ring[v % 2][:, 0, :], csil[:, 0:1], None, ALU.mult))
                for k in range(1, KD):
                    ins = STT(out=out, in0=ring[v % 2][:, k, :], scalar=csil[:, k:k + 1], in1=out, op0=ALU.mult, op1=ALU.add)
                    if k < KD - 1:
                        step(ins)
                ins.then_inc(mod_part, 1)

            def scale_col(q):
                s = (3 * q + 1) * KD
                g = V0["norm_g"] + 2 * q * KD
                STT(out=ncol[:, q, 0, :], in0=mod[:, s:s + KD], scalar=1.0, in1=vec[:, g:g + KD],
                    op0=ALU.add, op1=ALU.mult).then_inc(ncol_ready, 1)

            def gate_col(q):
                s = (3 * q + 2) * KD
                g = V0["norm_g"] + (2 * q + 1) * KD
                step(TT(ncol[:, q, 1, :], mod[:, s:s + KD], vec[:, g:g + KD], ALU.mult))

            def taps(out, src, name, j, width, free=None, wait=True):
                def col(k):
                    return V(name, j * width + k)
                step(TS(out, src, col(width - 1), None, ALU.mult))
                for d in range(1, width):
                    ins = STT(out=out[:, d:S], in0=src[:, 0:S - d], scalar=col(width - 1 - d), in1=out[:, d:S],
                              op0=ALU.mult, op1=ALU.add)
                    if d < width - 1 or free is None:
                        step(ins)
                if free is not None:
                    ins.then_inc(free, 1)

            nc.vector.memset(zcol[:], 0.0)
            nc.vector.memset(epscol[:], EPS)
            nc.vector.memset(acc[:], 0.0)
            nc.vector.memset(ones[:], 1.0).then_inc(const_ready, 1)
            dve.wait_ge(const_ready, 1)
            for k in range(KD):
                add_square(0, k)
            dve.wait_ge(csil_ready, 1)
            dve.wait_ge(vec_in, 48)
            for v in range(8):
                mod_unit(v, ada_a)
            mod_evac(6)
            mod_evac(7)
            dve.wait_ge(mod_out, 8)
            scale_col(0)
            norm_in(0, 0, "a_in")

            for j in range(8):
                t = T0["a_in"] + 3 * j
                for u in range(2):
                    mod_unit(8 + 2 * j + u, ada_a)
                read_out(t)
                done(C0["a_in"] + 3 * j + 1)
                ins = TT(ta[:, j % 2, :], ta[:, j % 2, :], psum[(t + 1) % 4][:], ALU.mult)
                ins.then_inc(bank_free[(t + 1) % 4], 1)
                dve.wait_ge(bank_free[(t + 1) % 4], (t + 1) // 4 + 1)
                taps(tb[:, j % 2, :], ta[:, j % 2, :], "a_conv", j, 3)
                done(C0["a_in"] + 3 * j + 2)
                TT(tb[:, j % 2, :], tb[:, j % 2, :], psum[(t + 2) % 4][:], ALU.mult).then_inc(bank_free[(t + 2) % 4], 1)
                lo_part(g_lo[:, j, :], tb[:, j % 2, :], g_hi[:, j, :], I0["a_out"] + j)
            mod_evac(22)
            mod_evac(23)
            dve.wait_ge(mod_out, 26)
            gate_col(0)
            scale_col(1)
            gate_col(1)
            clear_acc()
            with dve.Fori(0, 2) as it:
                for m in range(4):
                    add_square(1, m, it, 4)
            residual(0, 2)
            norm_in(1, 2, "f_in0")

            def ffn(n):
                f_in, f_out = f"f_in{n}", f"f_out{n}"

                def hidden(j, it, n):
                    c, t = C0[f_in] + 2 * j, T0[f_in] + 2 * j
                    read_out(t, it, 2 * n)
                    done(c + 1, it, 2 * n)
                    b = (t + 1) % 4
                    TT(tb[:, j % 2, :], ta[:, j % 2, :], psum[b][:], ALU.mult).then_inc(bank_free[b], 1)
                    lo_part(tile(g_lo, it * n + j), tb[:, j % 2, :], tile(g_hi, it * n + j), it * n + (I0[f_out] + j))

                if n == 0:
                    with dve.Fori(0, 4) as it:
                        step.loop(it, 6 * (KD - 1))
                        for j in range(4):
                            hidden(j, it, 4)
                            if j < 3:
                                for v in range(24 + 2 * j, 26 + 2 * j):
                                    mod_unit(v, ada_f, it)
                        step.end(4)
                    mod_evac(46)
                    mod_evac(47)
                    dve.wait_ge(mod_out, 52)
                    gate_col(1)
                    for q in range(2, 4):
                        scale_col(q)
                        gate_col(q)
                    with dve.Fori(0, 3) as it:
                        for j in range(16, 18):
                            hidden(j, it, 2)
                else:
                    with dve.Fori(0, 11) as it:
                        for j in range(2):
                            hidden(j, it, 2)
                clear_acc()
                with dve.Fori(0, 2) as it:
                    for m in range(4):
                        add_square(3 + 4 * n, m, it, 4)
                residual(1 + 2 * n, 4 + 4 * n)

            dve.wait_ge(brow_wr, 16)
            dve.wait_ge(hot_sum, 3)
            ffn(0)
            norm_in(2, 4, "m_in")

            done(C0["m_in"])
            b = T0["m_in"] % 4
            X, EXP, SERIES, SQUARE, SUM, MAX, DT = range(7)
            step(TS(dts[:, SUM, :], psum[b][0:HEADS, :], dtp[:, 0:1], None, ALU.add))
            STT(out=dts[:, X, :], in0=dts[:, SUM, :], scalar=-1.0, in1=dts[:, SUM, :], op0=ALU.mult, op1=ALU.min).then_inc(dt_lin, 1)
            TS(dts[:, MAX, :], dts[:, SUM, :], 0.0, None, ALU.max).then_inc(bank_free[b], 1)
            dve.wait_ge(dt_exp, 1)
            step(TS(dts[:, SERIES, :], dts[:, EXP, :], 2.0, None, ALU.add))
            step(nc.vector.reciprocal(dts[:, SERIES, :], dts[:, SERIES, :]))
            step(TT(dts[:, SERIES, :], dts[:, EXP, :], dts[:, SERIES, :], ALU.mult))
            step(TT(dts[:, SQUARE, :], dts[:, SERIES, :], dts[:, SERIES, :], ALU.mult))
            step(TS(dts[:, SUM, :], dts[:, SQUARE, :], 1.0 / 17, None, ALU.mult))
            for odd in range(15, 1, -2):
                step(STT(out=dts[:, SUM, :], in0=dts[:, SUM, :], scalar=1.0 / odd, in1=dts[:, SQUARE, :], op0=ALU.add, op1=ALU.mult))
            step(STT(out=dts[:, SUM, :], in0=dts[:, SUM, :], scalar=1.0, in1=dts[:, SERIES, :], op0=ALU.add, op1=ALU.mult))
            step(STT(out=dts[:, DT, :], in0=dts[:, SUM, :], scalar=2.0, in1=dts[:, MAX, :], op0=ALU.mult, op1=ALU.add))
            dve.wait_ge(a_exp, 1)
            step(TS(dts[:, X, :], dts[:, DT, :], dtp[:, 2:3], -1.0, ALU.mult, ALU.mult))
            step(nc.vector.memset(dts[:, EXP, :], 1.0))
            for i in range(NT):
                at = slice(i * P, (i + 1) * P)
                step(nc.vector.tensor_tensor_scan(cs[:, at], dts[:, EXP, at], dts[:, X, at], 0.0, ALU.mult, ALU.add))
            for i, (at, n) in OFF_COL.items():
                last = nc.vector.tensor_tensor_scan(cs[:, at:at + n], dts[:, EXP, (i + 1) * P:S], dts[:, X, (i + 1) * P:S],
                                                    cs[:, (i + 1) * P - 1:(i + 1) * P], ALU.mult, ALU.add)
            last.then_inc(cs_ready, 1)
            dve.wait_ge(tokT_done, 1)
            by_token = lambda bank: bank[:, 0:P].rearrange("p (i h) -> p i h", i=NT)
            nc.vector.tensor_copy(cs_tok[:], by_token(psum[4])).then_inc(tok_ready, 1)
            TS(ncs_tok[:], by_token(psum[4]), -1.0, None, ALU.mult).then_inc(tok_ready, 1)
            nc.vector.tensor_copy(dt_tok[:], by_token(psum[5])).then_inc(tok_ready, 1)
            dve.wait_ge(tok_ready, 3)

            def conv(G, s, it, n):
                t = T0["m_in"] + 1 + GSTEP * G + s
                done(C0["m_in"] + 1 + GSTEP * G + s, it, n * GSTEP)
                if 4 * G + s >= 2:
                    dve.wait_ge(grp_ready, 4 * G + s - 1 + it * (4 * n))
                taps(tb[:, s % 2, :], psum[t % 4][:], "m_conv", it * (4 * n) + (4 * G + s), 4, bank_free[t % 4])

            def epilogue(g, f, p, it, n):
                gi = g + it * n
                dve.wait_ge(y_done, gi * HPG + 2 * f + 2)
                STT(out=ta[:, f, :], in0=xg[:, p, f], scalar=V("m_d", gi * 2 + f), in1=psum[7 - f][:],
                    op0=ALU.mult, op1=ALU.add).then_inc(y_evac, 1)
                dve.wait_ge(y_evac, gi * 2 + f + 1)
                t = T0["m_in"] + 1 + GSTEP * g + 4 + f
                read_out(t, it, n * GSTEP)
                TT(ta[:, f, :], ta[:, f, :], zg[:, p, f], ALU.mult).then_inc(yt_done, 1)

            def group_sum(gi):
                dve.wait_ge(gsq_out, gi * 2 + 2)
                TT(sq[:, 0, :], sq[:, 0, :], sq[:, 1, :], ALU.add).then_inc(gacc, 1)

            def group_norm(gi):
                dve.wait_ge(gstd, gi + 1)
                step(nc.vector.reciprocal(rstd[:], rstd[:]))
                for f in range(2):
                    ins = STT(out=tile(y32, gi * 2 + f), in0=ta[:, f, :], scalar=V("m_norm", gi * 2 + f), in1=rstd[:],
                              op0=ALU.mult, op1=ALU.mult)
                ins.then_inc(y32_out, 1)

            def scaled_x(gi):
                dve.wait_ge(xT_done, gi + 1)
                for f in range(2):
                    h = gi * HPG + 2 * f
                    dt = dt_tok[:, :, h:h + 2] if isinstance(h, int) else dt_tok[:, :, bass.ds(h, 2)]
                    TT(xdt[:, :, f, :].rearrange("p i (r d) -> p i r d", r=2),
                       psum[4 + f][:].rearrange("p (i r d) -> p i r d", i=NT, r=2),
                       dt.unsqueeze(3).broadcast_to([P, NT, 2, 64]), ALU.mult).then_inc(xdt_done, 1)

            def segment(g, r, it, n):
                h = HPG * g + r + it * (HPG * n)
                dve.wait_ge(csb_in[r % 2], 16 * ((HPG * g + r) // 2 + 1) + it * (8 * HPG * n))
                if HPG * g + r >= 2:
                    dve.wait_ge(y_done, h - 1)
                d = eb[:, r % 2, 0:S]
                col = cs_tok[:, :, h:h + 1] if isinstance(h, int) else cs_tok[:, :, bass.ds(h, 1)]
                step(TT(d.rearrange("p (i l) -> p i l", i=NT), csb[:, r % 2, 0:S].rearrange("p (i l) -> p i l", i=NT),
                        col.broadcast_to([P, NT, P]), ALU.subtract))
                TS(d, d, 0.0, None, ALU.min).then_inc(seg_done, 1)

            def decayed(gi, r):
                dve.wait_ge(exp_done, gi * HPG + r + 1)
                if r == 0:
                    dve.wait_ge(cbm_act, gi * 2 + 2)
                TT(eb[:, r % 2, :], eb[:, r % 2, :], cbm[:], ALU.mult).then_inc(m_done, 1)

            def m_body(G, it, n, g, before, proj=True):
                gi, p = g + it * n, g % 2
                for s in range(GSTEP):
                    if s == 0 and before:
                        epilogue(g - 1, 1, 1 - p, it, n)
                        group_sum(gi - 1)
                    if s == 1:
                        if before:
                            group_norm(gi - 1)
                        scaled_x(gi)
                        segment(g, 0, it, n)
                    if s == 2:
                        dve.wait_ge(cb_done, gi + 1)
                        step(TT(cbm[:, 0:S].rearrange("p (i l) -> p i l", i=NT), psum[4][:].rearrange("p (i l) -> p i l", i=NT),
                                tri.unsqueeze(1).broadcast_to([P, NT, P]), ALU.mult))
                    if s >= 2:
                        decayed(gi, s - 2)
                    if 2 <= s <= 4:
                        segment(g, s - 1, it, n)
                    if s == 4:
                        epilogue(g, 0, p, it, n)
                    if proj and s < 4:
                        conv(G, s, it, n)

            for s in range(4):
                conv(0, s, 0, 0)
            m_body(1, 0, 0, 0, False)
            with dve.Fori(0, 3) as it:
                step.loop(it, 36)
                for b in range(2):
                    m_body(2 + b, it, 2, 1 + b, True)
                step.end(3)
            m_body(8, 0, 0, 7, True, proj=False)
            epilogue(7, 1, 1, 0, 0)
            group_sum(7)
            group_norm(7)
            for k in range(16):
                lo_part(g_lo[:, k, :], y32[:, k, :], g_hi[:, k, :], I0["m_out"] + k)
            clear_acc()
            with dve.Fori(0, 2) as it:
                for m in range(4):
                    add_square(5, m, it, 4)
            residual(2, 6)
            norm_in(3, 6, "f_in1")
            ffn(1)
            norm_in(4, 8, "w_in")

            dve.wait_ge(kc_in, 16 * 8)
            for kv, pos in enumerate(("pos_k", "pos_v")):
                if kv:
                    dve.wait_ge(blk_ready, kv)
                windows = kc2[:, kv].rearrange("p g (c j t) -> p j g c t", j=8, t=2)
                for half in range(2):
                    cols = vec[:, V0[pos] + 8 * half:V0[pos] + 8 * half + 8].unsqueeze(2).broadcast_to([P, 8, NCMP])
                    for e in range(2):
                        ins = TT(blk[:, 8 * half:8 * half + 8, e, :], windows[:, :, e, half:half + NCMP, 0], cols, ALU.add)
                ins.then_inc(blk_out, 1)
                dve.wait_ge(blk_split, kv + 1)
                TT(blk_lo[:], blk[:], blk_hi[:].bitcast(F32), ALU.subtract).then_inc(blk_ready, 1)

            dve.wait_ge(sink_in, 16)
            read_out(T0["w_in"] + 32)
            with dve.Fori(0, 4) as r:
                U = len(UNITS)
                step.loop(r, 98)

                def by_tile(u):
                    return prob_buf(u)[:, 0:P].rearrange("p (i c) -> p i c", i=NT)[:, :, 0:NCMP]

                def scored(u):
                    kind, e, qt = UNITS[u]
                    dve.wait_ge(score_done, r * U + u + 1)
                    if u == 0:
                        dve.wait_ge(bias_in, 64 * r + 64)
                    if u >= 3:
                        dve.wait_ge(tr_done, r * U + u - 2)
                    st, bank = stat[:, u % 2], psum[u % 2]
                    n = NT if kind == "C" else 1
                    if kind == "C":
                        for i in range(NT):
                            at = 3 * P + CMP - 1 - i * P
                            ins = STT(out=prob_buf(u)[:, i * 32:i * 32 + NCMP], in0=bank[:, i * 32:i * 32 + NCMP], scalar=0.125,
                                      in1=tbias[:, e, at:at + (NCMP - 1) * STRIDE + 1:STRIDE], op0=ALU.mult, op1=ALU.add)
                        src = by_tile(u)
                    else:
                        k0, k1 = span(kind, qt)
                        w = k1 - k0
                        bias = abias[:, e, TA - w:TA] if kind == "A" else tbias[:, e, S - w:S]
                        src = prob_buf(u)[:, 0:w]
                        ins = STT(out=src, in0=bank[:, 0:w], scalar=0.125, in1=bias, op0=ALU.mult, op1=ALU.add)
                    step(ins)
                    step(nc.vector.tensor_reduce(st[:, 0, 0:n], src, AX.X, ALU.max))
                    if kind == "A":
                        step(TT(st[:, 0, 0:1], st[:, 0, 0:1], sinkb[:, bass.ds(r + 4 * e, 1)], ALU.max))
                    TS(st[:, 1, 0:n], st[:, 0, 0:n], -1.0, None, ALU.mult).then_inc(soft_done, 1)

                def normalised(u):
                    kind, e, qt = UNITS[u]
                    dve.wait_ge(pexp_done, r * U + u + 1)
                    st = stat[:, u % 2]
                    n = NT if kind == "C" else 1
                    if kind == "A":
                        step(TT(st[:, 2, 0:1], st[:, 2, 0:1], st[:, 3, 0:1], ALU.add))
                    step(nc.vector.reciprocal(st[:, 4, 0:n], st[:, 2, 0:n]))
                    if kind == "C":
                        gate = gates[:, :, bass.ds(r * 3 + 12 * e, 1)].rearrange("p i a -> p (i a)")
                        step(TT(st[:, 4, :], st[:, 4, :], gate, ALU.mult))
                        step(TT(st[:, 4, :], st[:, 4, :], qvalid, ALU.mult))
                        TT(by_tile(u), by_tile(u), st[:, 4, :].unsqueeze(2).broadcast_to([P, NT, NCMP]), ALU.mult).then_inc(pn_done, 1)
                        return
                    k0, k1 = span(kind, qt)
                    p = prob_buf(u)[:, 0:k1 - k0]
                    if kind == "A":
                        TS(p, p, st[:, 4, 0:1], None, ALU.mult).then_inc(pn_done, 1)
                    else:
                        gate = gates[:, qt, bass.ds(r * 3 + (12 * e + 1 + "SW".index(kind)), 1)]
                        TS(p, p, st[:, 4, 0:1], gate, ALU.mult, ALU.mult).then_inc(pn_done, 1)

                for u in range(U + 1):
                    if u < U:
                        scored(u)
                    if u >= 1:
                        normalised(u - 1)
                for i in range(2):
                    lo_part(tile(h_lo, r + 4 * i), ta[:, i, :], tile(h_hi, r + 4 * i), r * 2 + (I0["up"] + i))
                dve.wait_ge(in_ready, r * 2 + (I0["up"] + 2))
                step.end(4)

            for u in range(8):
                done(C0["up"] + u)
                for i, buf in enumerate((ta, tb)):
                    t = T0["up"] + 2 * u + i
                    TT(buf[:, u % 2, :], psum[t % 4][:], ga[:, 8 * i + u, :], ALU.mult).then_inc(bank_free[t % 4], 1)
                dve.wait_ge(bank_free[t % 4], t // 4 + 1)
                TT(ta[:, u % 2, :], ta[:, u % 2, :], tb[:, u % 2, :], ALU.add).then_inc(prod_out, 1)
                lo_part(mg_lo[:, u, :], ta[:, u % 2, :], mg_hi[:, u, :], I0["w_out"] + u)
            clear_acc()
            with dve.Fori(0, 2) as it:
                for u in range(4):
                    b = (T0["w_out"] + u) % 4
                    done(C0["w_out"] + u, it, 4)
                    TT(tile(x, it * 4 + u), tile(x, it * 4 + u), psum[b][:], ALU.add).then_inc(bank_free[b], 1)
                    add_square(9, u, it, 4)
            norm_in(5, 9, "g_in")

            with dve.Fori(0, 11) as it:
                step.loop(it, 8)
                for j in range(2):
                    for i, buf in enumerate((ta, tb)):
                        t = T0["g_in"] + 2 * j + i
                        done(C0["g_in"] + 2 * j + i, it, 4)
                        taps(buf[:, j, :], psum[t % 4][:], "g_conv", it * 2 + (KF * i + j), 3, bank_free[t % 4])
                    dve.wait_ge(gate_out, it * 2 + (j + 1))
                    STT(out=ta[:, j, :], in0=ta[:, j, :], scalar=V("g_conv_b", it * 2 + j), in1=sq[:, j, :],
                        op0=ALU.add, op1=ALU.mult).then_inc(prod_out, 1)
                    lo_part(tile(g_lo, it * 2 + j), ta[:, j, :], tile(g_hi, it * 2 + j), it * 2 + (I0["g_out"] + j))
                step.end(11)
            clear_acc()
            for m in range(8):
                b = (T0["g_out"] + m) % 4
                done(C0["g_out"] + 4 * m + 3)
                TT(x[:, m, :], x[:, m, :], psum[b][:], ALU.add).then_inc(bank_free[b], 1)
                add_square(10, m)

            reciprocal(10)
            for k in range(KD):
                if k >= 2:
                    dve.wait_ge(out_done, 16 * (k - 1))
                STT(out=ta[:, k % 2, :], in0=x[:, k, :], scalar=V("norm_final", k), in1=rstd[:],
                    op0=ALU.mult, op1=ALU.mult).then_inc(out_ready, 1)


def bucket(dist):
    exact = BUCKETS // 2
    d = np.maximum(dist, 1).astype(np.float32)
    large = exact + (np.log(d / np.float32(exact)) / np.float32(np.log(128 / exact)) * np.float32(BUCKETS - exact)).astype(np.int32)
    return np.where(dist < exact, np.maximum(dist, 0), np.minimum(large, BUCKETS - 1))


def one_hot(dist, valid):
    rows = np.where(valid, bucket(dist), BUCKETS)
    return (np.arange(BUCKETS + 1)[:, None] == rows[None, :]).astype(np.float32)


def columns(v):
    return np.asarray(v).reshape(-1, P).T


def stationary(w):
    k, m = w.shape
    return w.reshape(k // P, P, m // P, P).transpose(2, 1, 0, 3).reshape(m // P, P, k)


def moving(w):
    k, n = w.shape
    return w.reshape(k // P, P, n).transpose(1, 0, 2).reshape(P, -1)


def halves(t):
    m = t.shape[0]
    return t.reshape(m, P, 2, KF // 2 * P).transpose(0, 2, 1, 3).reshape(2 * m, P, KF // 2 * P)


def interleave(*ts):
    return np.stack(ts, axis=1).reshape((-1,) + ts[0].shape[1:])


def taps_columns(w):
    width, n = w.shape
    return w.reshape(width, n // P, P).transpose(2, 1, 0).reshape(P, -1)


def by_group(t, n):
    x, b, c = t[:2 * GROUPS].reshape(GROUPS, 2, *t.shape[1:]), t[2 * GROUPS:3 * GROUPS][:, None], t[3 * GROUPS:4 * GROUPS][:, None]
    parts = [x, b, c]
    if n == 6:
        parts.append(t[4 * GROUPS:].reshape(GROUPS, 2, *t.shape[1:]))
    return np.concatenate(parts, axis=1).reshape(t.shape)


def head_pairs(n_first):
    return np.concatenate([np.arange(h * 64, h * 64 + 64) for r in range(4) for h in (r, r + 4)]) + n_first


def layout(a):
    ins = {}
    vecs = dict(c=columns(a["c"]), ada_b=columns(a["ada_b"]), norm_g=columns(a["norm_g"]),
                a_conv=taps_columns(a["a_conv_w"][0]),
                m_norm=columns(a["m_norm_g"]), m_d=columns(np.repeat(a["m_d"][0], 64)),
                pos_k=a["cmp_pos_k_2"][0].reshape(16, P).T, pos_v=a["cmp_pos_v_2"][0].reshape(16, P).T,
                norm_mix=columns(a["norm_mix_2"]), norm_ffn=columns(a["norm_ffn_2"]), norm_final=columns(a["norm_final_2"]),
                g_conv=taps_columns(a["conv_w_2"][0]), g_conv_b=columns(a["conv_b_2"]))
    conv = a["m_conv_w"][0].reshape(4, 4 * GROUPS, P).transpose(1, 2, 0)
    vecs["m_conv"] = by_group(conv, 4).transpose(1, 0, 2).reshape(P, -1)
    vecs["m_conv_b"] = by_group(a["m_conv_b"][0].reshape(4 * GROUPS, P), 4).T
    ins["vec"] = np.concatenate([vecs[n] for n in VCOLS], axis=1)
    qvalid = np.ones((P, NT))
    qvalid[:CMP - 1, 0] = 0
    ins["kst"] = np.concatenate([np.eye(P), np.triu(np.ones((P, P))), qvalid], axis=1).astype(np.float32)
    ins["dtp"] = np.stack([a["m_dt_bias"][0], a["m_a_log"][0]], axis=1)
    ins["x"] = moving(a["x"][0].T)
    ada = a["ada_w"]
    ins["ada"] = ada.reshape(KD, P, 48, 256).transpose(2, 1, 0, 3).reshape(48, P, KD * 256)
    b, c, v = (stationary(w) for w in np.split(a["a_w_in"][0], 3, axis=1))
    ins["a_in"] = interleave(c, v, b)
    ins["a_out"] = stationary(a["a_w_out"][0])
    for i in range(2):
        ins[f"f_in{i}"] = interleave(*(stationary(w) for w in np.split(a["f_w_in"][i], 2, axis=1)))
        ins[f"f_out{i}"] = halves(stationary(a["f_w_out"][i]))
    m = a["m_w_in"][0]
    z, xbc, dt = m[:, :16 * P], m[:, 16 * P:48 * P], m[:, 48 * P:]
    dt = np.concatenate([dt, np.zeros((D, P - HEADS), np.float32)], axis=1)
    mo = stationary(a["m_w_out"][0])
    ins["m"] = np.concatenate([stationary(dt), by_group(np.concatenate([stationary(xbc), stationary(z)]), 6),
                               mo.reshape(8, P, 2, D).transpose(0, 2, 1, 3).reshape(16, P, D)])
    w = a["w_in_2"][0]
    at = dict(zip("qa ka va qb kc vc ks vs kw vw gn ga gb".split(),
                  np.cumsum([0, 512, 128, 128, 512, 128, 128, 128, 128, 128, 128, 24, 1024])))
    part = lambda n, width=P: w[:, at[n]:at[n] + width]
    free = np.concatenate([w[:, head_pairs(at["qa"])], w[:, head_pairs(at["qb"])]] + [part(n) for n in "ka ks kw kc vc".split()]
                          + [part("ga", D), part("gb", D)], axis=1)
    gn = np.concatenate([moving(part("gn", 24)), np.zeros((P, D - KD * 24), np.float32)], axis=1)
    ins["w_in"] = np.concatenate([stationary(free), np.stack([moving(part(n)) for n in ("va", "vs", "vw")] + [gn])])
    ins["cmp"] = np.concatenate([stationary(a[n][0]).reshape(2, P, 2, D).transpose(0, 2, 1, 3).reshape(4, P, D)
                                 for n in ("cmp_w1_k_2", "cmp_w1_v_2")])
    ins["w2"] = np.stack([a[n][0].reshape(2, P, 64).transpose(1, 0, 2) for n in ("cmp_w2_k_2", "cmp_w2_v_2")])
    up = np.concatenate([a[n][0][head_pairs(0)] for n in ("w_up_a_2", "w_up_b_2")])
    ins["up"] = stationary(up)
    ins["w_out"] = stationary(a["w_out_2"][0])
    ins["g_in"] = interleave(*(stationary(w) for w in np.split(a["w_ffn_in_2"][0], 2, axis=1)))
    ins["g_out"] = halves(stationary(a["w_ffn_out_2"][0]))
    ins["tbl"] = np.concatenate([a["rel_bias_table_2"], np.full((1, 16), NEG, np.float32)])
    db, da = S - 1 - np.arange(WB), 2 * P - 1 - np.arange(WA)
    ins["hot"] = np.concatenate([one_hot(db, db >= 0), one_hot(da, (da >= 0) & (da < P))], axis=1)
    ins["sinks"] = a["attn_sinks_2"]
    return {n: np.ascontiguousarray(v) for n, v in ins.items()}


def kernel(**arrays):
    import concourse.bacc as bacc
    from concourse.bass_utils import run_bass_kernel_spmd
    ins = layout({n: np.asarray(v) for n, v in arrays.items()})
    nc = bacc.Bacc("TRN2", target_bir_lowering=False, num_devices=1)
    io = {n: nc.dram_tensor(n + "_d", v.shape, F32, kind="ExternalInput").ap() for n, v in ins.items()}
    io["out"] = nc.dram_tensor("out_d", [KD, P, S], F32, kind="ExternalOutput").ap()
    io["cs"] = nc.dram_tensor("cs_d", [HEADS, PACK], F32, kind="Internal").ap()
    io["brow"] = nc.dram_tensor("brow_d", [16, WB + WA], F32, kind="Internal").ap()
    io["rows"] = nc.dram_tensor("rows_d", [16, P * (WB + 1)], F32, kind="Internal").ap()
    program(nc, io)
    result = run_bass_kernel_spmd(nc, [{n + "_d": v for n, v in ins.items()}], core_ids=[0])
    out = result.results[0]["out_d"]
    return np.ascontiguousarray(out.reshape(D, S).T)[None]
```

```python
from contextlib import ExitStack

import numpy as np

import concourse.bass as bass
from concourse import mybir

F32 = mybir.dt.float32
F32R = mybir.dt.float32r
ACT = mybir.ActivationFunctionType
ALU = mybir.AluOpType
AX = mybir.AxisListType

P = 128
S = 512
NT = S // P
D = 1024
KD = D // P
FF = 2816
KF = FF // P
EPS = 1e-6
RING = 4
CH = 8
NEG = -1e30

GROUPS = 8
HPG = 4
HEADS = GROUPS * HPG
GSTEP = 6
PACK = 1280
OFF_COL = {0: (512, 384), 2: (896, 128), 1: (1024, 256)}

CMP, STRIDE = 32, 16
NCMP = (S - CMP) // STRIDE + 1
WB = 1024
TB = 896
WA = 384
TA = 256
BUCKETS = 32

CHUNKS = dict(a_in=24, a_out=8, f_in0=44, f_out0=32, m_in=1 + GROUPS * GSTEP, m_out=16,
              f_in1=44, f_out1=32, w_in=33 + 8, up=8, w_out=8, g_in=44, g_out=32)
TILES = dict(a_in=24, a_out=8, f_in0=44, f_out0=8, m_in=1 + GROUPS * GSTEP, m_out=8,
             f_in1=44, f_out1=8, w_in=33, up=16, w_out=8, g_in=44, g_out=8)
INS = dict(a_in=8, a_out=8, f_in0=8, f_out0=22, m_in=8, m_out=16, f_in1=8, f_out1=22, w_in=8,
           up=8, w_out=8, g_in=8, g_out=22)


def starts(sizes):
    at, out = 0, {}
    for name, n in sizes.items():
        out[name] = at
        at += n
    return out, at


CMP_AFTER = (22, 23, 24, 25, 28, 29, 30, 31)


def w_chunk(u):
    return u + sum(a < u for a in CMP_AFTER)


def cmp_chunk(i):
    return CMP_AFTER[i] + i + 1


C0, NCH = starts(CHUNKS)
T0, _ = starts(TILES)
I0, _ = starts(INS)

VCOLS = dict(c=8, ada_b=96, norm_g=64, a_conv=24, m_conv=128, m_conv_b=32, m_norm=16, m_d=16,
             pos_k=16, pos_v=16, norm_mix=8, norm_ffn=8, norm_final=8, g_conv=132, g_conv_b=44)
V0, NV = starts(VCOLS)
KCOLS = dict(ident=128, tri=128, qvalid=4)
K0, NK = starts(KCOLS)


UNITS = [u for e in range(2) for u in [("C", e, 0)] + [(k, e, q) for q in range(NT) for k in "ASW"]]
HALF = len(UNITS) // 2


def span(kind, qt):
    return (max(0, (qt - 1) * P) if kind == "A" else 0), (qt + 1) * P


def program(nc, io):
    with ExitStack() as ctx:
        def sem(name):
            return ctx.enter_context(nc.semaphore(name))

        def sb(name, shape, dt=F32):
            return ctx.enter_context(nc.sbuf_tensor(name, shape, dt))

        raw = sb("raw", [P, RING, CH, P])
        whi = sb("whi", [P, RING, CH, P], F32R)
        wlo = sb("wlo", [P, RING, CH, P], F32R)
        x = sb("x", [P, KD, S])
        vec = sb("vec", [P, NV])
        kst = sb("kst", [P, NK])
        ones = sb("ones", [P, P])
        mod = sb("mod", [P, 96])
        csil = sb("csil", [P, KD])
        ncol = sb("ncol", [P, 4, 2, KD])
        zcol = sb("zcol", [P, 1])
        epscol = sb("epscol", [P, 1])
        dtp = sb("dtp", [HEADS, 4])
        acc = sb("acc", [P, S])
        sq = sb("sq", [P, 2, S])
        rstd = sb("rstd", [P, S])
        ta = sb("ta", [P, 2, S])
        tb = sb("tb", [P, 2, S])
        modacc = sb("modacc", [P, 2, 256])
        ident = kst[:, K0["ident"]:K0["ident"] + P]
        tri = kst[:, K0["tri"]:K0["tri"] + P]
        qvalid = kst[:, K0["qvalid"]:K0["qvalid"] + NT]

        def V(name, j):
            if isinstance(j, int):
                return vec[:, V0[name] + j:V0[name] + j + 1]
            return vec[:, bass.ds(V0[name] + j, 1)]

        def view(at, name, shape, dt=F32):
            with ExitStack() as v:
                if at:
                    v.enter_context(nc.sbuf_tensor(f"pad_{name}", [P, at // 4], F32))
                return v.enter_context(nc.sbuf_tensor(name, shape, dt))

        KB = 1024
        H = 0
        G = 32 * KB
        h_hi = view(H, "h_hi", [P, KD, S], F32R)
        h_lo = view(H + 16 * KB, "h_lo", [P, KD, S], F32R)
        g_hi = view(G, "g_hi", [P, KF, S], F32R)
        g_lo = view(G + 44 * KB, "g_lo", [P, KF, S], F32R)
        y = view(H, "y", [P, KD, S])
        ada_a = [view(at, f"ada_a{i}", [P, KD, 256]) for i, at in enumerate((G + 16 * KB, G + 24 * KB))]
        ada_first = [view(at, f"ada_first{i}", [P, 2, KD, 256]) for i, at in enumerate((H, H + 16 * KB, G, G + 16 * KB))]
        ada_f = [view(at, f"ada_f{i}", [P, KD, 256]) for i, at in enumerate((G + 36 * KB, G + 80 * KB))]
        y32 = view(G + 44 * KB, "y32", [P, 16, S])
        xg = view(G, "xg", [P, 2, 2, S])
        bg = view(G + 8 * KB, "bg", [P, 2, S])
        cg = view(G + 12 * KB, "cg", [P, 2, S])
        zg = view(G + 16 * KB, "zg", [P, 2, 2, S])
        csb = view(G + 24 * KB, "csb", [P, 2, PACK])
        eb = view(G + 34 * KB, "eb", [P, 2, PACK])
        cbm = view(G + 76 * KB, "cbm", [P, PACK])
        dt_tok = view(G + 81 * KB, "dt_tok", [P, NT, HEADS])
        cs_tok = view(G + 81 * KB + 512, "cs_tok", [P, NT, HEADS])
        ncs_tok = view(G + 81 * KB + 1024, "ncs_tok", [P, NT, HEADS])
        xdt = view(G + 83 * KB, "xdt", [P, NT, 2, P])
        dts = view(G + 24 * KB, "dts", [HEADS, 7, S])
        cs = view(G + 76 * KB, "cs", [HEADS, PACK])
        ga = view(G, "ga", [P, 16, S])
        qk = view(G + 32 * KB, "qk", [P, 13, S])
        vab = view(G + 58 * KB, "vab", [P, 3, NT, P])
        tbias = view(G + 64 * KB, "tbias", [P, 2, TB])
        abias = view(G + 71 * KB, "abias", [P, 2, TA])
        kc2 = view(G + 73 * KB, "kc2", [P, 2, 2, S])
        kcmp = view(G + 81 * KB, "kcmp", [P, 32])
        vcmp = view(G + 81 * KB + 128, "vcmp", [32, P])
        hid = view(G + 81 * KB + 640, "hid", [P, 2, 2, 64])
        qst = view(G + 83 * KB, "qst", [P, 2, S])
        gates = view(G + 87 * KB, "gates", [P, NT, 24])
        sinkb = view(G + 87 * KB + 384, "sinkb", [P, 8])
        stat = view(G + 87 * KB + 448, "stat", [P, 4, 8, NT])
        blk = view(G + 64 * KB, "blk", [P, 16, 2, NCMP])
        blk_hi = view(G + 68 * KB, "blk_hi", [P, 16, 2, NCMP], F32R)
        blk_lo = view(G + 83 * KB, "blk_lo", [P, 16, 2, NCMP], F32R)
        w2 = rstd[:, 0:256].rearrange("p (a m d) -> p a m d", a=2, m=2)
        hot = view(G + 62 * KB, "hot", [BUCKETS + 1, WB + WA])
        brow = view(G + 68 * KB, "brow", [16, WB + WA])
        tbl = view(G + 74 * KB, "tbl", [BUCKETS + 1, 16])
        mg_hi = view(G + 32 * KB, "mg_hi", [P, KD, S], F32R)
        mg_lo = view(G + 48 * KB, "mg_lo", [P, KD, S], F32R)

        psum = [ctx.enter_context(nc.psum_tensor(f"bank{b}", [P, S], F32)) for b in range(8)]

        raw_in = [sem(f"raw_in{s}") for s in range(RING)]
        hi_ready, lo_ready, chunk_done = sem("hi_ready"), sem("lo_ready"), sem("chunk_done")
        bank_free = [sem(f"bank_free{b}") for b in range(4)]
        in_hi, in_ready = sem("in_hi"), sem("in_ready")
        x_in, vec_in, const_ready, csil_ready, out_ready, out_done = (
            sem(n) for n in ("x_in", "vec_in", "const_ready", "csil_ready", "out_ready", "out_done"))
        first_in = [sem(f"first_in{p}") for p in range(4)]
        ada_in = [sem("ada_in0"), sem("ada_in1")]
        mod_part, mod_sum, mod_out, ncol_ready = (sem(n) for n in ("mod_part", "mod_sum", "mod_out", "ncol_ready"))
        sq_out, acc_done, sum_done, std_out, x_done, t_out = (
            sem(n) for n in ("sq_out", "acc_done", "sum_done", "std_out", "x_done", "t_out"))
        dve_step = sem("dve_step")
        y_scaled = sem("y_scaled")
        gate_out, prod_out = sem("gate_out"), sem("prod_out")
        dt_lin, dt_exp, a_exp, cs_ready, cs_out, tokT_done, tok_ready = (
            sem(n) for n in ("dt_lin", "dt_exp", "a_exp", "cs_ready", "cs_out", "tokT_done", "tok_ready"))
        grp_ready, xT_done, xdt_done, cb_done, cbm_dve, cbm_act = (
            sem(n) for n in ("grp_ready", "xT_done", "xdt_done", "cb_done", "cbm_dve", "cbm_act"))
        csb_in = [sem("csb_in0"), sem("csb_in1")]
        seg_done, exp_done, m_done, y_done, y_evac, yt_done, gsq_out, gacc, gsum, gstd, y32_out = (
            sem(n) for n in ("seg_done", "exp_done", "m_done", "y_done", "y_evac", "yt_done", "gsq_out", "gacc",
                             "gsum", "gstd", "y32_out"))
        vt_done, v_out = sem("vt_done"), sem("v_out")
        tbl_in, hot_sum, brow_out, brow_wr, rows_wr, sink_in, w2_in = (
            sem(n) for n in ("tbl_in", "hot_sum", "brow_out", "brow_wr", "rows_wr", "sink_in", "w2_in"))
        bias_in = [sem("bias_in0"), sem("bias_in1")]
        kc_in, blk_out, blk_split, blk_ready, hid_out, cmp_sum, cmp_out = (
            sem(n) for n in ("kc_in", "blk_out", "blk_split", "blk_ready", "hid_out", "cmp_sum", "cmp_out"))
        q_st, score_done, soft_done, pexp_done, pn_done, tr_done, pt_done, pv_done = (
            sem(n) for n in ("q_st", "score_done", "soft_done", "pexp_done", "pn_done", "tr_done", "pt_done", "pv_done"))

        block = ctx.enter_context(nc.Block())

        def tile(t, j):
            if isinstance(j, int):
                return t[:, j, :]
            return t[:, bass.ds(j, 1), :].rearrange("p a n -> p (a n)")

        def score_bank(u):
            return psum[(0, 1, 4, 7)[u % 4]]

        def stage(i):
            return (tb[:, 0, :], tb[:, 1, :], ta[:, 0, :], ta[:, 1, :])[i]

        def prob_buf(u):
            return (ta[:, 0, :], ta[:, 1, :], sq[:, 0, :], sq[:, 1, :])[u % 4]

        def turn(c, it, n):
            return c // RING + it * (n // RING)

        class Chain:

            def __init__(self, eng, steps):
                self.eng, self.steps, self.v, self.it, self.per = eng, steps, 0, 0, 0

            def loop(self, it, per):
                self.it, self.per, self.base = it, per, self.v

            def end(self, times):
                assert self.v - self.base == self.per, (self.v - self.base, self.per)
                self.v = self.base + times * self.per
                self.it = self.per = 0

            def note(self, ins):
                self.v += 1
                ins.then_inc(self.steps, 1)
                return self.v

            def wait(self, v):
                self.eng.wait_ge(self.steps, v + self.it * self.per)

            def __call__(self, ins):
                self.wait(self.note(ins))


        X_SUMS = (2, 4, 6, 8)

        @block.sync
        def _(sp):
            def load(src, c, it=0, n=0, cols=CH * P):
                s = c % RING
                if c >= RING:
                    sp.wait_ge(lo_ready, c - RING + 1 + it * n)
                dst = raw[:, s].rearrange("p k m -> p (k m)")[:, 0:cols]
                sp.dma_start(dst, src).then_inc(raw_in[s], 16)

            def at(w, i):
                if isinstance(i, int):
                    return w[i]
                return w[bass.ds(i, 1)].rearrange("a p n -> (a p) n")

            def ada(ring, v, i):
                sp.wait_ge(mod_part, i - 1)
                sp.dma_start(ring[v % 2].rearrange("p k n -> p (k n)"), at(io["ada"], i)).then_inc(ada_in[v % 2], 16)

            sp.dma_start(vec[:], io["vec"]).then_inc(vec_in, 16)
            sp.dma_start(x[:], io["x"].rearrange("p (k n) -> p k n", k=KD)).then_inc(x_in, 16)
            sp.dma_start(kst[:], io["kst"]).then_inc(vec_in, 16)
            sp.dma_start(dtp[:, 0:2], io["dtp"]).then_inc(vec_in, 16)
            sp.dma_start(tbl[:], io["tbl"]).then_inc(tbl_in, 16)
            sp.dma_start(hot[:], io["hot"]).then_inc(tbl_in, 16)
            for v in range(8):
                sp.dma_start(ada_first[v // 2][:, v % 2].rearrange("p k n -> p (k n)"), io["ada"][v]).then_inc(first_in[v // 2], 16)
                if v < 4:
                    load(io["a_in"][v], v)
            for j in range(8):
                for s in range(3):
                    c = 3 * j + s
                    if c >= 4:
                        load(io["a_in"][c], c)
                if j:
                    for u in range(2):
                        ada(ada_a, u, 6 + 2 * j + u)
                if j == 5:
                    sp.wait_ge(brow_out, 3)
                    sp.dma_start(io["brow"], brow[:]).then_inc(brow_wr, 16)
                if j >= 6:
                    sp.wait_ge(brow_wr, 16)
                    for hh in range(8 * (j - 6), 8 * (j - 5)):
                        n0, w = (0, WB) if hh >= 8 else (WB, WA)
                        dst = io["rows"][hh, 0:P * (w + 1)].rearrange("(p w) -> p w", p=P)[:, 0:w]
                        sp.dma_start(dst, io["brow"][hh:hh + 1, n0:n0 + w].broadcast_to([P, w])).then_inc(rows_wr, 16)

            def uniform(name):
                n = CHUNKS[name]
                with sp.Fori(0, n // RING) as it:
                    for u in range(RING):
                        load(at(io[name], it * RING + u), C0[name] + u, it, RING)
                for u in range(n - n % RING, n):
                    load(io[name][u], C0[name] + u)

            def pairs(name):
                with sp.Fori(0, 2) as it:
                    for m in range(4):
                        for u in range(4):
                            w = at(io[name], it * 8 + 2 * m + u // 2)
                            lo, hi = ((0, 6 * P), (6 * P, 11 * P))[u % 2]
                            load(w[:, lo:hi], C0[name] + 4 * m + u, it, 16, hi - lo)

            uniform("a_out")
            for u in range(2):
                ada(ada_a, u, 22 + u)
            def chunks(it, n, first, last):
                for u in range(first, last):
                    load(at(io["f_in0"], it * n + u), C0["f_in0"] + u, it, n)

            def pair(v, it=0, n=0):
                for u in range(2):
                    ada(ada_f, v + u, it * n + (v + u))

            def turn_of(it, first, last):
                chunks(it, 8, first, first + 3)
                pair(26 + 6 * (first // 8 - 1), it, 6)
                chunks(it, 8, first + 3, first + 5)
                pair(28 + 6 * (first // 8 - 1), it, 6)
                chunks(it, 8, first + 5, first + 7)
                if not last:
                    pair(30 + 6 * (first // 8 - 1), it, 6)
                chunks(it, 8, first + 7, first + 8)

            chunks(0, 0, 0, 8)
            pair(24)
            with sp.Fori(0, 3) as it:
                turn_of(it, 8, False)
            turn_of(0, 32, True)
            chunks(0, 0, 40, CHUNKS["f_in0"])
            pairs("f_out0")

            def mixer_weights(i, it=0, n=0):
                load(at(io["m"], i + it * n), C0["m_in"] + i, it, n)

            def decay_row(r, h, first=False):
                if not first:
                    sp.wait_ge(exp_done, h - 1)
                src = io["cs"][h:h + 1, :] if isinstance(h, int) else io["cs"][bass.ds(h, 1), :]
                sp.dma_start(csb[:, r % 2, :], src.broadcast_to([P, PACK])).then_inc(csb_in[r % 2], 16)

            def body(G, it=0, n=0):
                c = 1 + GSTEP * (G + 1)
                h = HPG * (G - 1) + it * (HPG * n)
                mixer_weights(c + 1, it, GSTEP * n)
                for s in range(HPG):
                    mixer_weights(c + 2 + s, it, GSTEP * n)
                    decay_row(s, h + 2 + s)
                mixer_weights(c + GSTEP, it, GSTEP * n)

            for c in range(1 + GSTEP):
                mixer_weights(c)
            sp.wait_ge(cs_ready, 1)
            sp.dma_start(io["cs"], cs[:]).then_inc(cs_out, 16)
            for c in range(1 + GSTEP, 4 + GSTEP):
                mixer_weights(c)
            sp.wait_ge(cs_out, 16)
            sp.wait_ge(tok_ready, 3)
            for r in range(2):
                decay_row(r, r, True)
            for c in range(4 + GSTEP, 2 + 2 * GSTEP):
                mixer_weights(c)
            body(1)
            with sp.Fori(0, 3) as it:
                for b in range(2):
                    body(2 + b, it, 2)
            for r in range(2, HPG):
                decay_row(r, HPG * (GROUPS - 1) + r)
            for c in range(2 + GSTEP * (GROUPS + 1), CHUNKS["m_in"] + CHUNKS["m_out"]):
                mixer_weights(c)
            uniform("f_in1")
            pairs("f_out1")
            uniform("w_in")
            uniform("up")
            uniform("w_out")
            uniform("g_in")
            pairs("g_out")
            for k in range(KD):
                sp.wait_ge(out_ready, k + 1)
                sp.dma_start(io["out"][k], ta[:, k % 2, :]).then_inc(out_done, 16)
                sp.wait_ge(out_done, 16 * (k + 1))

        @block.gpsimd
        def _(pool):
            def split_lo(c, it=0):
                s = c % RING
                pool.wait_ge(hi_ready, c + 1 + it * RING)
                nc.gpsimd.tensor_tensor(wlo[:, s], raw[:, s], whi[:, s].bitcast(F32), ALU.subtract).then_inc(lo_ready, 1)

            with pool.Fori(0, NCH // RING) as it:
                for u in range(RING):
                    split_lo(u, it)
            for c in range(NCH - NCH % RING, NCH):
                split_lo(c)

        @block.tensor
        def _(pe):
            PRODUCTS = ((whi, "hi"), (whi, "lo"), (wlo, "hi"))

            def chunk(c, it, n, bank, ktiles, k0, xs, first, last, wait_in=None):
                s = c % RING
                pe.wait_ge(lo_ready, c + 1 + it * n)
                for kk in range(ktiles):
                    k = k0 + kk
                    if wait_in is not None:
                        pe.wait_ge(in_ready, wait_in + k + 1)
                    for i, (w, part) in enumerate(PRODUCTS):
                        mm = nc.tensor.matmul(psum[bank][:], w[:, s, kk, :], xs[part == "lo"][:, k, :],
                                              start=first and kk == 0 and i == 0,
                                              stop=last and kk == ktiles - 1 and i == 2)
                mm.then_inc(chunk_done, 1)

            def bank_of(t, it=0, n=0):
                b = t % 4
                if t >= 4:
                    pe.wait_ge(bank_free[b], t // 4 + it * (n // 4))
                return b

            def single(name, u, it=0, n=0, xs=(h_hi, h_lo), wait=True, c=None):
                b = bank_of(T0[name] + u, it, n)
                chunk(C0[name] + (u if c is None else c), it, n, b, CH, 0, xs, True, True, I0[name] if wait else None)

            def two(name, u, it=0, n=0):
                banks = [bank_of(T0[name] + u + i, it, n) for i in range(2)]
                pe.wait_ge(lo_ready, C0[name] + u + 2 + it * n)
                for k in range(KD):
                    pe.wait_ge(in_ready, I0[name] + k + 1)
                    for i in range(2):
                        for j, (w, part) in enumerate(PRODUCTS):
                            mm = nc.tensor.matmul(psum[banks[i]][:], w[:, (C0[name] + u + i) % RING, k, :],
                                                  (h_hi, h_lo)[part == "lo"][:, k, :],
                                                  start=k == 0 and j == 0, stop=k == KD - 1 and j == 2)
                        if k == KD - 1:
                            mm.then_inc(chunk_done, 1)

            def down(name, it, xs):
                for m in range(4):
                    b = bank_of(T0[name] + m, it, 4)
                    k = 0
                    for u, n in enumerate((6, 5, 6, 5)):
                        chunk(C0[name] + 4 * m + u, it, 16, b, n, k, xs, u == 0, u == 3, I0[name] if m == 0 else None)
                        k += n

            def column_sums(n):
                pe.wait_ge(acc_done, KD * (n + 1))
                nc.tensor.matmul(psum[4][:], ones[:], acc[:], start=True, stop=True).then_inc(sum_done, 1)

            def x_sums(n):
                for k in range(KD):
                    pe.wait_ge(sq_out, KD * n + k + 1)
                    nc.tensor.matmul(psum[4][:], ones[:], sq[:, k % 2, :], start=k == 0, stop=k == KD - 1).then_inc(acc_done, 1)

            def modulation(v, i):
                pe.wait_ge(mod_part, i + 1)
                for b in range(2):
                    mm = nc.tensor.matmul(psum[5 + 2 * (v % 2)][:, b:b + 1], modacc[:, v % 2, b * P:(b + 1) * P],
                                          ones[:, 0:1], start=True, stop=True)
                mm.then_inc(mod_sum, 1)

            pe.wait_ge(const_ready, 1)
            column_sums(0)
            for p in range(4):
                pe.wait_ge(mod_part, 2 * (p + 1))
                for b in range(4):
                    mm = nc.tensor.matmul(psum[5][:, 4 * p + b:4 * p + b + 1], stage(p)[:, b * P:(b + 1) * P], ones[:, 0:1],
                                          start=True, stop=True)
                mm.then_inc(mod_sum, 2)
            for j in range(8):
                if j == 0:
                    two("a_in", 0)
                for s in range(0 if j else 2, 3):
                    single("a_in", 3 * j + s)
                if j < 3:
                    if j == 0:
                        pe.wait_ge(tbl_in, 32)
                    else:
                        pe.wait_ge(brow_out, j)
                    e = min(S, WB + WA - S * j)
                    nc.tensor.matmul(psum[6][0:16, 0:e], tbl[:], hot[:, S * j:S * j + e], start=True, stop=True).then_inc(hot_sum, 1)
                if 1 <= j < 7:
                    for u in range(2):
                        modulation(u, 6 + 2 * j + u)
            for u in range(KD):
                single("a_out", u, xs=(g_hi, g_lo))
                if u == 1:
                    for v in range(20, 22):
                        modulation(v, v)
            for v in range(22, 24):
                modulation(v, v)
            column_sums(1)
            x_sums(2)

            def ffn(n):
                if n == 0:
                    with pe.Fori(0, 4) as it:
                        two("f_in0", 0, it, 8)
                        for u in range(2, 8):
                            single("f_in0", u, it, 8, wait=False)
                            if u in (3, 5, 7):
                                for v in range(24 + u - 3, 24 + u - 1):
                                    modulation(v, it * 6 + v)
                    with pe.Fori(0, 3) as it:
                        for u in range(4):
                            single("f_in0", 32 + u, it, 4, wait=False)
                else:
                    with pe.Fori(0, 11) as it:
                        two("f_in1", 0, it, 4)
                        for u in range(2, 4):
                            single("f_in1", u, it, 4, wait=False)
                with pe.Fori(0, 2) as it:
                    down(f"f_out{n}", it, (g_hi, g_lo))
                column_sums(3 + 4 * n)
                x_sums(4 + 4 * n)

            ffn(0)

            two("m_in", 0)
            def ssd_sum(g):
                pe.wait_ge(gacc, g + 1)
                nc.tensor.matmul(psum[6][:], ones[:], sq[:, 0, :], start=True, stop=True).then_inc(gsum, 1)

            def ssd_turn(g, p):
                pe.wait_ge(grp_ready, 4 * (g + 1))
                for f in range(2):
                    for i in range(NT):
                        mm = nc.tensor.transpose(psum[4 + f][:, i * P:(i + 1) * P], xg[:, p, f, i * P:(i + 1) * P], ident)
                mm.then_inc(xT_done, 1)

            def ssd_cb(g, p):
                pe.wait_ge(xdt_done, 2 * (g + 1))
                for i in range(NT):
                    nc.tensor.matmul(psum[4][:, i * P:(i + 1) * P], bg[:, p, i * P:(i + 1) * P], cg[:, p, i * P:(i + 1) * P],
                                     start=True, stop=True)
                for i, b, col in ((0, 5, 0), (2, 5, 384), (1, 6, 0)):
                    n = OFF_COL[i][1]
                    mm = nc.tensor.matmul(psum[b][:, col:col + n], bg[:, p, i * P:(i + 1) * P], cg[:, p, (i + 1) * P:S],
                                          start=True, stop=True)
                mm.then_inc(cb_done, 1)

            def ssd_y(g, r, h):
                pe.wait_ge(m_done, h + 1)
                bank = psum[7 if r < 2 else 6]
                rows = slice(64 * (r % 2), 64 * (r % 2) + 64)
                for i in range(NT):
                    w = xdt[:, i, r // 2, 64 * (r % 2):64 * (r % 2) + 64]
                    mm = nc.tensor.matmul(bank[rows, i * P:(i + 1) * P], w, eb[:, r % 2, i * P:(i + 1) * P],
                                          start=i == 0, stop=i == NT - 1, skip_group_check=True)
                    if i in OFF_COL:
                        at, n = OFF_COL[i]
                        mm = nc.tensor.matmul(bank[rows, (i + 1) * P:S], w, eb[:, r % 2, at:at + n],
                                              start=False, stop=False, skip_group_check=True)
                mm.then_inc(y_done, 1)

            def m_body(G, it, n, g, gn, before, proj=True):
                def proj_chunk(s):
                    if proj:
                        single("m_in", 1 + GSTEP * G + s, it, n, wait=False)
                p = g % 2
                gi = g + it * gn
                hi = HPG * g + it * (gn * HPG)
                proj_chunk(0)
                if before:
                    ssd_sum(gi - 1)
                ssd_turn(gi, p)
                proj_chunk(1)
                if before:
                    pe.wait_ge(gstd, gi)
                ssd_cb(gi, p)
                for r in range(HPG):
                    proj_chunk(2 + r)
                    if r == 0 and before:
                        pe.wait_ge(y_evac, gi * 2)
                    if r == 2:
                        pe.wait_ge(cbm_act, (gi + 1) * 2)
                    ssd_y(gi, r, hi + r)

            for s in range(1, GSTEP):
                single("m_in", 1 + s, wait=False)
            pe.wait_ge(cs_ready, 1)
            for i in range(NT):
                nc.tensor.transpose(psum[4][:, i * HEADS:(i + 1) * HEADS], cs[:, i * P:(i + 1) * P], ident[0:HEADS, 0:HEADS])
                mm = nc.tensor.transpose(psum[5][:, i * HEADS:(i + 1) * HEADS], dts[:, 6, i * P:(i + 1) * P], ident[0:HEADS, 0:HEADS])
            mm.then_inc(tokT_done, 1)
            pe.wait_ge(tok_ready, 3)
            m_body(1, 0, 0, 0, 0, False)
            with pe.Fori(0, 3) as it:
                for b in range(2):
                    m_body(2 + b, it, 2 * GSTEP, 1 + b, 2, True)
            m_body(8, 0, 0, 7, 0, True, proj=False)
            ssd_sum(7)
            with pe.Fori(0, 2) as it:
                for m in range(4):
                    b = bank_of(T0["m_out"] + m, it, 4)
                    for u in range(2):
                        chunk(C0["m_out"] + 2 * m + u, it, 8, b, CH, CH * u, (g_hi, g_lo), u == 0, u == 1, I0["m_out"])
            column_sums(5)
            x_sums(6)
            ffn(1)

            with pe.Fori(0, 3) as it:
                two("w_in", 0, it, 4)
                for u in range(2, 4):
                    single("w_in", u, it, 4, wait=False)
            def compress(i):
                kv, m, half = i // 4, i // 2 % 2, i % 2
                pe.wait_ge(blk_ready, kv + 1)
                pe.wait_ge(v_out, 4)
                c = C0["w_in"] + cmp_chunk(i)
                pe.wait_ge(lo_ready, c + 1)
                for kk in range(CH):
                    for j, (w, part) in enumerate(PRODUCTS):
                        src = (blk_hi, blk_lo)[part == "lo"]
                        mm = nc.tensor.matmul(psum[4 + kv][:, m * 64:m * 64 + 2 * NCMP], w[:, c % RING, kk, :],
                                              src[:, CH * half + kk].rearrange("p g c -> p (g c)"),
                                              start=half == 0 and kk == 0 and j == 0, stop=half == 1 and kk == CH - 1 and j == 2)
                mm.then_inc(chunk_done, 1)

            for u in range(12, 33):
                single("w_in", u, wait=False, c=w_chunk(u))
                if u in CMP_AFTER:
                    compress(CMP_AFTER.index(u))
                if u in range(15, 19):
                    i = u - 15
                    t = T0["w_in"] + 13 + i
                    pe.wait_ge(bank_free[t % 4], t // 4 + 1)
                    if i >= 2:
                        pe.wait_ge(v_out, i - 1)
                    rows = P if i < 3 else 24
                    for q in range(NT):
                        mm = nc.tensor.transpose(psum[4 + i % 2][:, q * P:q * P + rows], stage(i)[0:rows, q * P:(q + 1) * P],
                                                 ident[0:rows, 0:rows])
                    mm.then_inc(vt_done, 1)

            pe.wait_ge(w2_in, 32)
            pe.wait_ge(hid_out, 2)
            for e in range(2):
                for m in range(2):
                    nc.tensor.matmul(psum[6][64 * e:64 * e + 64, 0:NCMP], w2[:, 0, m, :], hid[:, 0, m, e * NCMP:(e + 1) * NCMP],
                                     start=m == 0, stop=m == 1)
            for e in range(2):
                for m in range(2):
                    mm = nc.tensor.matmul(psum[7][0:NCMP, 64 * e:64 * e + 64], hid[:, 1, m, e * NCMP:(e + 1) * NCMP], w2[:, 1, m, :],
                                          start=m == 0, stop=m == 1)
            mm.then_inc(cmp_sum, 1)

            pe.wait_ge(cmp_out, 2)
            pe.wait_ge(v_out, 4)
            for b in range(4):
                pe.wait_ge(bank_free[b], (T0["up"] - 1 - b) // 4 + 1)
            with pe.Fori(0, 4) as r:
                U = len(UNITS)

                def scores(u):
                    kind, e, qt = UNITS[u]
                    rows = slice(64 * e, 64 * e + 64)
                    bank = score_bank(u)
                    if u == 0:
                        pe.wait_ge(q_st, 2 * r + 2)
                    if u >= 4:
                        pe.wait_ge(soft_done, r * U + u - 3)
                    if kind == "C":
                        for i in range(NT):
                            mm = nc.tensor.matmul(bank[:, i * 32:i * 32 + NCMP], qst[rows, 1, i * P:(i + 1) * P], kcmp[rows, 0:NCMP],
                                                  start=True, stop=True)
                    else:
                        k = qk[rows, 8 + "ASW".index(kind), :]
                        k0, k1 = span(kind, qt)
                        mm = nc.tensor.matmul(bank[:, 0:k1 - k0], qst[rows, int(kind != "A"), qt * P:(qt + 1) * P], k[:, k0:k1],
                                              start=True, stop=True)
                    mm.then_inc(score_done, 1)

                def turn_probs(u):
                    kind, e, qt = UNITS[u]
                    bank = psum[2 + u % 2]
                    pe.wait_ge(pn_done, r * U + u + 1)
                    if u >= 2:
                        pe.wait_ge(pt_done, r * U + u - 1)
                    sp_ = prob_buf(u)
                    if kind == "C":
                        for i in range(NT):
                            mm = nc.tensor.transpose(bank[0:NCMP, i * P:(i + 1) * P], sp_[:, i * 32:i * 32 + NCMP], ident)
                    else:
                        k0, k1 = span(kind, qt)
                        for i in range((k1 - k0) // P):
                            mm = nc.tensor.transpose(bank[:, i * P:(i + 1) * P], sp_[:, i * P:(i + 1) * P], ident)
                    mm.then_inc(tr_done, 1)

                def values(u):
                    kind, e, qt = UNITS[u]
                    rows = slice(64 * e, 64 * e + 64)
                    bank = psum[5 if kind == "A" else 6]
                    pe.wait_ge(pt_done, r * U + u + 1)
                    pt = tb[:, u % 2, :]
                    if kind == "C":
                        mm = nc.tensor.matmul(bank[rows, :], vcmp[0:NCMP, 64 * e:64 * e + 64], pt[0:NCMP, :],
                                              start=True, stop=False, skip_group_check=True)
                    else:
                        k0, k1 = span(kind, qt)
                        for i in range((k1 - k0) // P):
                            mm = nc.tensor.matmul(bank[rows, qt * P:(qt + 1) * P],
                                                  vab[:, "ASW".index(kind), k0 // P + i, 64 * e:64 * e + 64],
                                                  pt[:, i * P:(i + 1) * P], start=kind == "A" and i == 0, stop=False,
                                                  skip_group_check=True)
                    mm.then_inc(pv_done, 1)

                for u in range(4):
                    scores(u)
                for u in range(U):
                    if u + 4 < U:
                        scores(u + 4)
                    turn_probs(u)
                    if u >= 1:
                        values(u - 1)
                values(U - 1)

            for u in range(8):
                c = C0["up"] + u
                for half in range(2):
                    b = bank_of(T0["up"] + 2 * u + half)
                    if u == 0 and half == 0:
                        pe.wait_ge(lo_ready, c + 1)
                    elif half == 0:
                        pe.wait_ge(lo_ready, c + 1)
                    for kk in range(4):
                        k = 4 * half + kk
                        pe.wait_ge(in_ready, I0["up"] + 8)
                        for i, (w, part) in enumerate(PRODUCTS):
                            mm = nc.tensor.matmul(psum[b][:], w[:, c % RING, k, :], (h_hi, h_lo)[part == "lo"][:, k, :],
                                                  start=kk == 0 and i == 0, stop=kk == 3 and i == 2)
                mm.then_inc(chunk_done, 1)
            with pe.Fori(0, 2) as it:
                for u in range(4):
                    single("w_out", u, it, 4, (mg_hi, mg_lo))
            column_sums(9)
            with pe.Fori(0, 11) as it:
                two("g_in", 0, it, 4)
                for u in range(2, 4):
                    single("g_in", u, it, 4, wait=False)
            with pe.Fori(0, 2) as it:
                down("g_out", it, (g_hi, g_lo))
            column_sums(10)

        @block.scalar
        def _(act):
            def split_hi(c, it=0, n=0):
                if isinstance(it, int) and c + it * n >= NCH:
                    return
                s = c % RING
                act.wait_ge(raw_in[s], 16 * (turn(c, it, n) + 1))
                if c >= RING:
                    act.wait_ge(chunk_done, c - RING + 1 + it * n)
                nc.scalar.activation(whi[:, s], raw[:, s], ACT.Copy).then_inc(hi_ready, 1)

            def done(c, it=0, n=0):
                act.wait_ge(chunk_done, c + 1 + it * n)

            def read_out(t, it=0, n=0):
                act.wait_ge(bank_free[t % 4], t // 4 + 1 + it * (n // 4))

            def root(n):
                if n in X_SUMS:
                    act.wait_ge(acc_done, KD * (n + 1))
                else:
                    act.wait_ge(sum_done, n + 1 - sum(i < n for i in X_SUMS))
                nc.scalar.activation(rstd[:], psum[4][:], ACT.Sqrt, bias=epscol[:], scale=1.0 / D).then_inc(std_out, 1)

            def square(src, n, k, it=0, per=0):
                if KD * n + k >= 2:
                    act.wait_ge(acc_done, KD * n + k - 1 + it * per)
                nc.scalar.activation(sq[:, k % 2, :], src, ACT.Square).then_inc(sq_out, 1)

            def x_squares(n, r):
                for k in range(KD):
                    act.wait_ge(x_done, KD * r + k + 1)
                    square(x[:, k, :], n, k)

            def norm_out(i, phase, a, b):
                for k in range(KD):
                    act.wait_ge(t_out, KD * i + k + 1)
                    if k >= 2:
                        act.wait_ge(in_ready, I0[phase] + k - 1)
                    nc.scalar.activation(tb[:, k % 2, :], ta[:, k % 2, :], ACT.Identity, bias=b(k), scale=a(k))
                    nc.scalar.activation(h_hi[:, k, :], ta[:, k % 2, :], ACT.Identity, bias=b(k), scale=a(k)).then_inc(in_hi, 1)

            def mod_norm(i, phase, q):
                norm_out(i, phase, lambda k: ncol[:, q, 0, k:k + 1], lambda k: mod[:, 3 * q * KD + k:3 * q * KD + k + 1])

            def plain_norm(i, phase, name):
                norm_out(i, phase, lambda k: V(name, k), lambda k: zcol[:])

            def y_tile(name, n, m, chunks, it=0):
                c = C0[name] + m * chunks
                for u in range(chunks - 1):
                    split_hi(c + RING + u, it, 4 * chunks)
                done(c + chunks - 1, it, 4 * chunks)
                b = (T0[name] + m) % 4
                square(psum[b][:], n, m, it, 4)
                nc.scalar.activation(tile(y, it * 4 + m), psum[b][:], ACT.Copy).then_inc(bank_free[b], 1)
                split_hi(c + RING + chunks - 1, it, 4 * chunks)

            act.wait_ge(vec_in, 48)
            nc.scalar.activation(csil[:], vec[:, V0["c"]:V0["c"] + KD], ACT.Silu).then_inc(csil_ready, 1)
            nc.scalar.activation(dtp[:, 2:3], dtp[:, 1:2], ACT.Exp).then_inc(a_exp, 1)
            act.wait_ge(x_in, 16)
            act.wait_ge(const_ready, 1)
            for k in range(KD):
                square(x[:, k, :], 0, k)
            root(0)
            for c in range(RING):
                split_hi(c)
            act.wait_ge(ncol_ready, 1)
            mod_norm(0, "a_in", 0)

            for j in range(8):
                c, t = C0["a_in"] + 3 * j, T0["a_in"] + 3 * j
                done(c)
                nc.scalar.activation(ta[:, j % 2, :], psum[t % 4][:], ACT.Copy).then_inc(bank_free[t % 4], 1)
                if 1 <= j <= 3:
                    act.wait_ge(hot_sum, j)
                    e = min(S * j, WB + WA)
                    nc.scalar.activation(brow[:, S * (j - 1):e], psum[6][0:16, 0:e - S * (j - 1)], ACT.Copy).then_inc(brow_out, 1)
                for u in range(3):
                    split_hi(c + RING + u)
                read_out(t + 2)
                nc.scalar.activation(g_hi[:, j, :], tb[:, j % 2, :], ACT.Copy).then_inc(in_hi, 1)
            with act.Fori(0, 2) as it:
                for m in range(4):
                    y_tile("a_out", 1, m, 1, it)
            root(1)
            x_squares(2, 0)
            root(2)
            act.wait_ge(ncol_ready, 2)
            mod_norm(1, "f_in0", 1)

            def ffn(n):
                f_in, f_out = f"f_in{n}", f"f_out{n}"
                with act.Fori(0, 11) as it:
                    for u in range(0, 4, 2):
                        c, t, j = C0[f_in] + u, T0[f_in] + u, u // 2
                        done(c, it, 4)
                        nc.scalar.activation(ta[:, j, :], psum[t % 4][:], ACT.Silu).then_inc(bank_free[t % 4], 1)
                        split_hi(c + RING, it, 4)
                        split_hi(c + RING + 1, it, 4)
                        read_out(t + 1, it, 4)
                        nc.scalar.activation(tile(g_hi, it * 2 + j), tb[:, j, :], ACT.Copy).then_inc(in_hi, 1)
                with act.Fori(0, 2) as it:
                    for m in range(4):
                        y_tile(f_out, 3 + 4 * n, m, 4, it)
                root(3 + 4 * n)
                x_squares(4 + 4 * n, 1 + 2 * n)
                root(4 + 4 * n)

            ffn(0)
            act.wait_ge(ncol_ready, 4)
            mod_norm(2, "m_in", 2)

            act.wait_ge(dt_lin, 1)
            nc.scalar.activation(dts[:, 1, :], dts[:, 0, :], ACT.Exp).then_inc(dt_exp, 1)
            split_hi(C0["m_in"] + RING)

            def conv_silu(G, s, it, n):
                t = T0["m_in"] + 1 + GSTEP * G + s
                read_out(t, it, n * GSTEP)
                dst = (xg[:, G % 2, 0], xg[:, G % 2, 1], bg[:, G % 2], cg[:, G % 2])[s]
                bias = V("m_conv_b", it * (4 * n) + 4 * G + s)
                if s == 0 and G >= 2:
                    act.wait_ge(yt_done, 2 * (G - 1) + it * (2 * n))
                nc.scalar.activation(dst, tb[:, s % 2, :], ACT.Silu, bias=bias).then_inc(grp_ready, 1)

            def evac(G, s, it, n):
                c, t = C0["m_in"] + 1 + GSTEP * G + s, T0["m_in"] + 1 + GSTEP * G + s
                if 1 <= s <= 4:
                    conv_silu(G, s - 1, it, n)
                if s >= 4:
                    done(c, it, n * GSTEP)
                    nc.scalar.activation(zg[:, G % 2, s - 4], psum[t % 4][:], ACT.Silu).then_inc(bank_free[t % 4], 1)
                split_hi(c + RING, it, n * GSTEP)

            def ssd_exp(h, r):
                act.wait_ge(csb_in[r % 2], 16 * (h // 2 + 1) if isinstance(h, int) else 16 * (h[0] // 2 + 1) + h[1] * (8 * h[2]))
                hv = h if isinstance(h, int) else h[0] + h[1] * h[2]
                if not (isinstance(h, int) and h < 2):
                    act.wait_ge(y_done, hv - 1)
                for i, (at, n) in OFF_COL.items():
                    bias = ncs_tok[:, i, hv:hv + 1] if isinstance(hv, int) else ncs_tok[:, i, bass.ds(hv, 1)]
                    nc.scalar.activation(eb[:, r % 2, at:at + n], csb[:, r % 2, at:at + n], ACT.Exp, bias=bias)
                act.wait_ge(seg_done, hv + 1)
                nc.scalar.activation(eb[:, r % 2, 0:S], eb[:, r % 2, 0:S], ACT.Exp).then_inc(exp_done, 1)

            def group_square(g, f):
                act.wait_ge(yt_done, g * 2 + f + 1)
                nc.scalar.activation(sq[:, f, :], ta[:, f, :], ACT.Square).then_inc(gsq_out, 1)

            def group_root(g):
                act.wait_ge(gsum, g + 1)
                nc.scalar.activation(rstd[:], psum[6][:], ACT.Sqrt, bias=epscol[:], scale=1.0 / 256).then_inc(gstd, 1)

            def m_body(G, it, n, g, before, proj=True):
                gi = g + it * n
                head = lambda r: HPG * g + r if isinstance(it, int) else (HPG * g + r, it, HPG * n)
                for s in range(GSTEP):
                    if s == 0 and before:
                        group_square(gi - 1, 1)
                    if s == 1:
                        if before:
                            group_root(gi - 1)
                        ssd_exp(head(0), 0)
                    if s == 2:
                        act.wait_ge(cb_done, gi + 1)
                        if before:
                            act.wait_ge(m_done, gi * HPG)
                        nc.scalar.activation(cbm[:, S:2 * S], psum[5][:], ACT.Copy).then_inc(cbm_act, 1)
                        nc.scalar.activation(cbm[:, 2 * S:PACK], psum[6][:, 0:PACK - 2 * S], ACT.Copy).then_inc(cbm_act, 1)
                    if 2 <= s <= 4:
                        ssd_exp(head(s - 1), s - 1)
                    if s == 4:
                        group_square(gi, 0)
                    if proj:
                        evac(G, s, it, n)

            for s in range(GSTEP):
                evac(0, s, 0, 0)
            act.wait_ge(tok_ready, 3)
            m_body(1, 0, 0, 0, False)
            with act.Fori(0, 3) as it:
                for b in range(2):
                    m_body(2 + b, it, 2, 1 + b, True)
            m_body(8, 0, 0, 7, True, proj=False)
            group_square(7, 1)
            group_root(7)
            act.wait_ge(y32_out, GROUPS)
            for k in range(16):
                nc.scalar.activation(g_hi[:, k, :], y32[:, k, :], ACT.Copy).then_inc(in_hi, 1)
            with act.Fori(0, 2) as it:
                for m in range(4):
                    y_tile("m_out", 5, m, 2, it)
            root(5)
            x_squares(6, 2)
            root(6)
            mod_norm(3, "f_in1", 3)
            ffn(1)
            plain_norm(4, "w_in", "norm_mix")

            with act.Fori(0, 3) as it:
                for u in range(4):
                    c, b = C0["w_in"] + u, (T0["w_in"] + u) % 4
                    done(c, it, 4)
                    nc.scalar.activation(tile(qk, it * 4 + u), psum[b][:], ACT.Copy).then_inc(bank_free[b], 1)
                    split_hi(c + RING, it, 4)
            act.dma_start(sinkb[:], io["sinks"].broadcast_to([P, 8])).then_inc(sink_in, 16)
            for u in range(12, 33):
                c, b = C0["w_in"] + w_chunk(u), (T0["w_in"] + u) % 4
                done(c)
                if u == 12:
                    nc.scalar.activation(qk[:, 12, :], psum[b][:], ACT.Copy).then_inc(bank_free[b], 1)
                elif u < 16:
                    nc.scalar.activation(stage(u - 13), psum[b][:], ACT.Copy).then_inc(bank_free[b], 1)
                elif u == 16:
                    nc.scalar.activation(stage(3)[0:24, :], psum[b][0:24, :], ACT.Sigmoid).then_inc(bank_free[b], 1)
                else:
                    nc.scalar.activation(ga[:, u - 17, :], psum[b][:], ACT.Sigmoid).then_inc(bank_free[b], 1)
                if u == 14:
                    for kv in range(2):
                        b = (T0["w_in"] + 11 + kv) % 4
                        act.wait_ge(bank_free[b], (T0["w_in"] + 11 + kv) // 4 + 1)
                        for e in range(2):
                            src = qk[64 * e:64 * e + 64, 11 + kv, :]
                            act.dma_start(kc2[0:64, kv, e, :], src).then_inc(kc_in, 16)
                            act.dma_start(kc2[64:128, kv, e, 0:S - 1], src[:, 1:S]).then_inc(kc_in, 16)
                if u in range(16, 20):
                    i = u - 16
                    act.wait_ge(vt_done, i + 1)
                    turned = psum[4 + i % 2][:].rearrange("p (q n) -> p q n", q=NT)
                    if i < 3:
                        nc.scalar.activation(vab[:, i], turned, ACT.Copy).then_inc(v_out, 1)
                    else:
                        nc.scalar.activation(gates[:], turned[:, :, 0:24], ACT.Copy).then_inc(v_out, 1)
                if u in (20, 26):
                    act.wait_ge(blk_out, (u - 20) // 6 + 1)
                    if u == 26:
                        done(C0["w_in"] + cmp_chunk(3))
                    nc.scalar.activation(blk_hi[:], blk[:], ACT.Copy).then_inc(blk_split, 1)
                split_hi(c + RING)
                if u in CMP_AFTER:
                    i = CMP_AFTER.index(u)
                    split_hi(c + 1 + RING)
                    if i % 4 == 3:
                        kv = i // 4
                        done(C0["w_in"] + cmp_chunk(i))
                        nc.scalar.activation(hid[:, kv, :, 0:2 * NCMP],
                                             psum[4 + kv][:, 0:P].rearrange("p (m c) -> p m c", m=2)[:, :, 0:2 * NCMP],
                                             ACT.Gelu_apprx_tanh).then_inc(hid_out, 1)
            for kv in range(2):
                act.dma_start(w2[:, kv], io["w2"][kv]).then_inc(w2_in, 16)
            act.wait_ge(cmp_sum, 1)
            nc.scalar.activation(kcmp[:, 0:NCMP], psum[6][:, 0:NCMP], ACT.Copy).then_inc(cmp_out, 1)
            nc.scalar.activation(vcmp[0:NCMP, :], psum[7][0:NCMP, 0:P], ACT.Copy).then_inc(cmp_out, 1)

            act.wait_ge(sink_in, 16)
            act.wait_ge(rows_wr, 16 * 16)
            def load_bias(e, r):
                for first, w, n, dst in ((8, WB, TB, tbias), (0, WA, TA, abias)):
                    h = first + 4 * e + r
                    src = io["rows"][h:h + 1] if isinstance(h, int) else io["rows"][bass.ds(h, 1)]
                    src = src[:, P - 1:P - 1 + P * w].rearrange("a (p w) -> (a p) w", p=P)[:, 0:n]
                    act.dma_start(dst[:, e, :], src).then_inc(bias_in[e], 16)

            load_bias(0, 0)
            with act.Fori(0, 4) as r:
                U = len(UNITS)
                load_bias(1, r)
                for i in range(2):
                    nc.scalar.activation(qst[:, i, :], tile(qk, r + 4 * i), ACT.Copy).then_inc(q_st, 1)

                def probs(u):
                    kind, e, qt = UNITS[u]
                    act.wait_ge(soft_done, r * U + u + 1)
                    st, p = stat[:, u % 4], prob_buf(u)
                    if kind == "C":
                        for i in range(NT):
                            last = nc.scalar.activation(p[:, i * 32:i * 32 + NCMP], p[:, i * 32:i * 32 + NCMP], ACT.Exp,
                                                        bias=st[:, 1, i:i + 1], accum_out=st[:, 2, i:i + 1])
                    else:
                        k0, k1 = span(kind, qt)
                        last = nc.scalar.activation(p[:, 0:k1 - k0], p[:, 0:k1 - k0], ACT.Exp, bias=st[:, 1, 0:1],
                                                    accum_out=st[:, 2, 0:1])
                    if kind == "A":
                        last = nc.scalar.activation(st[:, 3, 0:1], sinkb[:, bass.ds(r + 4 * e, 1)], ACT.Exp, bias=st[:, 1, 0:1])
                    last.then_inc(pexp_done, 1)
                    if u == HALF - 1:
                        load_bias(0, r + 1)

                def turned(u):
                    kind, e, qt = UNITS[u]
                    act.wait_ge(tr_done, r * U + u + 1)
                    if u >= 2:
                        act.wait_ge(pv_done, r * U + u - 1)
                    rows, n = (NCMP, S) if kind == "C" else (P, span(kind, qt)[1] - span(kind, qt)[0])
                    nc.scalar.activation(tb[0:rows, u % 2, 0:n], psum[2 + u % 2][0:rows, 0:n], ACT.Copy).then_inc(pt_done, 1)

                for u in range(U + 2):
                    if u < U:
                        probs(u)
                    if u >= 2:
                        turned(u - 2)
                act.wait_ge(pv_done, (r + 1) * U)
                for i in range(2):
                    nc.scalar.activation(ta[:, i, :], psum[5 + i][:], ACT.Copy)
                    nc.scalar.activation(tile(h_hi, r + 4 * i), psum[5 + i][:], ACT.Copy).then_inc(in_hi, 1)

            for u in range(8):
                act.wait_ge(prod_out, u + 1)
                nc.scalar.activation(mg_hi[:, u, :], ta[:, u % 2, :], ACT.Copy).then_inc(in_hi, 1)
                split_hi(C0["up"] + u + RING)
            with act.Fori(0, 2) as it:
                for u in range(4):
                    split_hi(C0["w_out"] + u + RING, it, 4)
                    read_out(T0["w_out"] + u, it, 4)
                    square(tile(x, it * 4 + u), 9, u, it, 4)
            root(9)
            plain_norm(5, "g_in", "norm_ffn")
            with act.Fori(0, 11) as it:
                for u in range(0, 4, 2):
                    c, t, j = C0["g_in"] + u, T0["g_in"] + u, u // 2
                    split_hi(c + RING, it, 4)
                    split_hi(c + RING + 1, it, 4)
                    read_out(t + 1, it, 4)
                    nc.scalar.activation(sq[:, j, :], tb[:, j, :], ACT.Silu, bias=V("g_conv_b", it * 2 + (KF + j))).then_inc(gate_out, 1)
                    act.wait_ge(prod_out, KD + it * 2 + (j + 1))
                    nc.scalar.activation(tile(g_hi, it * 2 + j), ta[:, j, :], ACT.Copy).then_inc(in_hi, 1)
            for m in range(8):
                for u in range(4):
                    split_hi(C0["g_out"] + 4 * m + u + RING)
                read_out(T0["g_out"] + m)
                square(x[:, m, :], 10, m)
            root(10)

        @block.vector
        def _(dve):
            TT, TS, STT = nc.vector.tensor_tensor, nc.vector.tensor_scalar, nc.vector.scalar_tensor_tensor
            step = Chain(dve, dve_step)

            def done(c, it=0, n=0):
                dve.wait_ge(chunk_done, c + 1 + it * n)

            def read_out(t, it=0, n=0):
                dve.wait_ge(bank_free[t % 4], t // 4 + 1 + it * (n // 4))

            def lo_part(dst, whole, hi, i):
                dve.wait_ge(in_hi, i + 1)
                TT(dst, whole, hi.bitcast(F32), ALU.subtract).then_inc(in_ready, 1)

            def clear_acc():
                step(nc.vector.memset(acc[:], 0.0))

            def add_square(n, k, it=0, per=0):
                dve.wait_ge(sq_out, KD * n + k + 1 + it * per)
                if KD * n + k:
                    dve.wait_ge(acc_done, KD * n + k + it * per)
                TT(acc[:], acc[:], sq[:, k % 2, :], ALU.add).then_inc(acc_done, 1)

            def reciprocal(n):
                dve.wait_ge(std_out, n + 1)
                step(nc.vector.reciprocal(rstd[:], rstd[:]))

            def residual(r, n):
                reciprocal(n - 1)
                for k in range(KD + 1):
                    if k < KD:
                        if k >= 2:
                            dve.wait_ge(x_done, KD * r + k - 1)
                        TT(ta[:, k % 2, :], y[:, k, :], rstd[:], ALU.mult).then_inc(y_scaled, 1)
                    if k >= 1:
                        dve.wait_ge(y_scaled, KD * r + k)
                        STT(out=x[:, k - 1, :], in0=ta[:, (k - 1) % 2, :], scalar=ncol[:, r, 1, k - 1:k], in1=x[:, k - 1, :],
                            op0=ALU.mult, op1=ALU.add).then_inc(x_done, 1)

            def norm_in(i, n, phase):
                reciprocal(n)
                for k in range(KD + 1):
                    if k < KD:
                        if k >= 2:
                            dve.wait_ge(in_hi, I0[phase] + k - 1)
                        TT(ta[:, k % 2, :], x[:, k, :], rstd[:], ALU.mult).then_inc(t_out, 1)
                    if k >= 1:
                        lo_part(h_lo[:, k - 1, :], tb[:, (k - 1) % 2, :], h_hi[:, k - 1, :], I0[phase] + k - 1)

            def mod_evac(v, it=0):
                i = v + it * 6
                dve.wait_ge(mod_sum, i + 1)
                dst, b = ((mod[:, 2 * v:2 * v + 2], vec[:, V0["ada_b"] + 2 * v:V0["ada_b"] + 2 * v + 2]) if isinstance(it, int)
                          else (mod[:, bass.ds(i * 2, 2)], vec[:, bass.ds(i * 2 + V0["ada_b"], 2)]))
                TT(dst, psum[5 + 2 * (v % 2)][:, 0:2], b, ALU.add).then_inc(mod_out, 1)

            def mod_unit(v, ring, it=0):
                if v >= 10:
                    mod_evac(v - 2, it)
                dve.wait_ge(ada_in[v % 2], 16 * (v // 2 - 3) + it * (16 * 3))
                out = modacc[:, v % 2, :]
                step(TS(out, ring[v % 2][:, 0, :], csil[:, 0:1], None, ALU.mult))
                for k in range(1, KD):
                    ins = STT(out=out, in0=ring[v % 2][:, k, :], scalar=csil[:, k:k + 1], in1=out, op0=ALU.mult, op1=ALU.add)
                    if k < KD - 1:
                        step(ins)
                ins.then_inc(mod_part, 1)

            def scale_col(q):
                s = (3 * q + 1) * KD
                g = V0["norm_g"] + 2 * q * KD
                STT(out=ncol[:, q, 0, :], in0=mod[:, s:s + KD], scalar=1.0, in1=vec[:, g:g + KD],
                    op0=ALU.add, op1=ALU.mult).then_inc(ncol_ready, 1)

            def gate_col(q):
                s = (3 * q + 2) * KD
                g = V0["norm_g"] + (2 * q + 1) * KD
                step(TT(ncol[:, q, 1, :], mod[:, s:s + KD], vec[:, g:g + KD], ALU.mult))

            def taps(out, src, name, j, width, free=None, wait=True):
                def col(k):
                    return V(name, j * width + k)
                step(TS(out, src, col(width - 1), None, ALU.mult))
                for d in range(1, width):
                    ins = STT(out=out[:, d:S], in0=src[:, 0:S - d], scalar=col(width - 1 - d), in1=out[:, d:S],
                              op0=ALU.mult, op1=ALU.add)
                    if d < width - 1 or free is None:
                        step(ins)
                if free is not None:
                    ins.then_inc(free, 1)

            nc.vector.memset(zcol[:], 0.0)
            nc.vector.memset(epscol[:], EPS)
            nc.vector.memset(acc[:], 0.0)
            nc.vector.memset(ones[:], 1.0).then_inc(const_ready, 1)
            dve.wait_ge(const_ready, 1)
            for k in range(KD):
                add_square(0, k)
            dve.wait_ge(csil_ready, 1)
            dve.wait_ge(vec_in, 48)
            for p in range(4):
                dve.wait_ge(first_in[p], 32)
                out = stage(p).rearrange("p (a n) -> p a n", a=2)
                step(TS(out, ada_first[p][:, :, 0, :], csil[:, 0:1], None, ALU.mult))
                for k in range(1, KD):
                    ins = STT(out=out, in0=ada_first[p][:, :, k, :], scalar=csil[:, k:k + 1], in1=out, op0=ALU.mult, op1=ALU.add)
                    if k < KD - 1:
                        step(ins)
                ins.then_inc(mod_part, 2)
            dve.wait_ge(mod_sum, 8)
            TT(mod[:, 0:16], psum[5][:, 0:16], vec[:, V0["ada_b"]:V0["ada_b"] + 16], ALU.add).then_inc(mod_out, 8)
            dve.wait_ge(mod_out, 8)
            scale_col(0)
            norm_in(0, 0, "a_in")

            for j in range(8):
                t = T0["a_in"] + 3 * j
                read_out(t)
                done(C0["a_in"] + 3 * j + 1)
                ins = TT(ta[:, j % 2, :], ta[:, j % 2, :], psum[(t + 1) % 4][:], ALU.mult)
                ins.then_inc(bank_free[(t + 1) % 4], 1)
                dve.wait_ge(bank_free[(t + 1) % 4], (t + 1) // 4 + 1)
                taps(tb[:, j % 2, :], ta[:, j % 2, :], "a_conv", j, 3)
                done(C0["a_in"] + 3 * j + 2)
                TT(tb[:, j % 2, :], tb[:, j % 2, :], psum[(t + 2) % 4][:], ALU.mult).then_inc(bank_free[(t + 2) % 4], 1)
                lo_part(g_lo[:, j, :], tb[:, j % 2, :], g_hi[:, j, :], I0["a_out"] + j)
                for u in range(2):
                    mod_unit(8 + 2 * j + u, ada_a)
            clear_acc()
            with dve.Fori(0, 2) as it:
                for m in range(4):
                    add_square(1, m, it, 4)
            mod_evac(22)
            mod_evac(23)
            dve.wait_ge(mod_out, 24)
            gate_col(0)
            scale_col(1)
            residual(0, 2)
            norm_in(1, 2, "f_in0")

            def ffn(n):
                f_in, f_out = f"f_in{n}", f"f_out{n}"

                def hidden(j, it, n):
                    c, t = C0[f_in] + 2 * j, T0[f_in] + 2 * j
                    read_out(t, it, 2 * n)
                    done(c + 1, it, 2 * n)
                    b = (t + 1) % 4
                    TT(tb[:, j % 2, :], ta[:, j % 2, :], psum[b][:], ALU.mult).then_inc(bank_free[b], 1)
                    lo_part(tile(g_lo, it * n + j), tb[:, j % 2, :], tile(g_hi, it * n + j), it * n + (I0[f_out] + j))

                if n == 0:
                    with dve.Fori(0, 4) as it:
                        step.loop(it, 6 * (KD - 1))
                        for j in range(4):
                            hidden(j, it, 4)
                            if j < 3:
                                for v in range(24 + 2 * j, 26 + 2 * j):
                                    mod_unit(v, ada_f, it)
                        step.end(4)
                    mod_evac(46)
                    mod_evac(47)
                    dve.wait_ge(mod_out, 50)
                    gate_col(1)
                    for q in range(2, 4):
                        scale_col(q)
                        gate_col(q)
                    with dve.Fori(0, 3) as it:
                        for j in range(16, 18):
                            hidden(j, it, 2)
                else:
                    with dve.Fori(0, 11) as it:
                        for j in range(2):
                            hidden(j, it, 2)
                clear_acc()
                with dve.Fori(0, 2) as it:
                    for m in range(4):
                        add_square(3 + 4 * n, m, it, 4)
                residual(1 + 2 * n, 4 + 4 * n)

            dve.wait_ge(brow_wr, 16)
            dve.wait_ge(hot_sum, 3)
            ffn(0)
            norm_in(2, 4, "m_in")

            done(C0["m_in"])
            b = T0["m_in"] % 4
            X, EXP, SERIES, SQUARE, SUM, MAX, DT = range(7)
            step(TS(dts[:, SUM, :], psum[b][0:HEADS, :], dtp[:, 0:1], None, ALU.add))
            STT(out=dts[:, X, :], in0=dts[:, SUM, :], scalar=-1.0, in1=dts[:, SUM, :], op0=ALU.mult, op1=ALU.min).then_inc(dt_lin, 1)
            TS(dts[:, MAX, :], dts[:, SUM, :], 0.0, None, ALU.max).then_inc(bank_free[b], 1)
            dve.wait_ge(dt_exp, 1)
            step(TS(dts[:, SERIES, :], dts[:, EXP, :], 2.0, None, ALU.add))
            step(nc.vector.reciprocal(dts[:, SERIES, :], dts[:, SERIES, :]))
            step(TT(dts[:, SERIES, :], dts[:, EXP, :], dts[:, SERIES, :], ALU.mult))
            step(TT(dts[:, SQUARE, :], dts[:, SERIES, :], dts[:, SERIES, :], ALU.mult))
            step(TS(dts[:, SUM, :], dts[:, SQUARE, :], 1.0 / 17, None, ALU.mult))
            for odd in range(15, 1, -2):
                step(STT(out=dts[:, SUM, :], in0=dts[:, SUM, :], scalar=1.0 / odd, in1=dts[:, SQUARE, :], op0=ALU.add, op1=ALU.mult))
            step(STT(out=dts[:, SUM, :], in0=dts[:, SUM, :], scalar=1.0, in1=dts[:, SERIES, :], op0=ALU.add, op1=ALU.mult))
            step(STT(out=dts[:, DT, :], in0=dts[:, SUM, :], scalar=2.0, in1=dts[:, MAX, :], op0=ALU.mult, op1=ALU.add))
            dve.wait_ge(a_exp, 1)
            step(TS(dts[:, X, :], dts[:, DT, :], dtp[:, 2:3], -1.0, ALU.mult, ALU.mult))
            step(nc.vector.memset(dts[:, EXP, :], 1.0))
            for i in range(NT):
                at = slice(i * P, (i + 1) * P)
                step(nc.vector.tensor_tensor_scan(cs[:, at], dts[:, EXP, at], dts[:, X, at], 0.0, ALU.mult, ALU.add))
            for i, (at, n) in OFF_COL.items():
                last = nc.vector.tensor_tensor_scan(cs[:, at:at + n], dts[:, EXP, (i + 1) * P:S], dts[:, X, (i + 1) * P:S],
                                                    cs[:, (i + 1) * P - 1:(i + 1) * P], ALU.mult, ALU.add)
            last.then_inc(cs_ready, 1)
            def conv(G, s, it, n):
                t = T0["m_in"] + 1 + GSTEP * G + s
                done(C0["m_in"] + 1 + GSTEP * G + s, it, n * GSTEP)
                if 4 * G + s >= 2:
                    dve.wait_ge(grp_ready, 4 * G + s - 1 + it * (4 * n))
                taps(tb[:, s % 2, :], psum[t % 4][:], "m_conv", it * (4 * n) + (4 * G + s), 4, bank_free[t % 4])

            def epilogue(g, f, p, it, n):
                gi = g + it * n
                dve.wait_ge(y_done, gi * HPG + 2 * f + 2)
                STT(out=ta[:, f, :], in0=xg[:, p, f], scalar=V("m_d", gi * 2 + f), in1=psum[7 - f][:],
                    op0=ALU.mult, op1=ALU.add).then_inc(y_evac, 1)
                dve.wait_ge(y_evac, gi * 2 + f + 1)
                t = T0["m_in"] + 1 + GSTEP * g + 4 + f
                read_out(t, it, n * GSTEP)
                TT(ta[:, f, :], ta[:, f, :], zg[:, p, f], ALU.mult).then_inc(yt_done, 1)

            def group_sum(gi):
                dve.wait_ge(gsq_out, gi * 2 + 2)
                TT(sq[:, 0, :], sq[:, 0, :], sq[:, 1, :], ALU.add).then_inc(gacc, 1)

            def group_norm(gi):
                dve.wait_ge(gstd, gi + 1)
                step(nc.vector.reciprocal(rstd[:], rstd[:]))
                for f in range(2):
                    ins = STT(out=tile(y32, gi * 2 + f), in0=ta[:, f, :], scalar=V("m_norm", gi * 2 + f), in1=rstd[:],
                              op0=ALU.mult, op1=ALU.mult)
                ins.then_inc(y32_out, 1)

            def scaled_x(gi):
                dve.wait_ge(xT_done, gi + 1)
                for f in range(2):
                    h = gi * HPG + 2 * f
                    dt = dt_tok[:, :, h:h + 2] if isinstance(h, int) else dt_tok[:, :, bass.ds(h, 2)]
                    TT(xdt[:, :, f, :].rearrange("p i (r d) -> p i r d", r=2),
                       psum[4 + f][:].rearrange("p (i r d) -> p i r d", i=NT, r=2),
                       dt.unsqueeze(3).broadcast_to([P, NT, 2, 64]), ALU.mult).then_inc(xdt_done, 1)

            def segment(g, r, it, n):
                h = HPG * g + r + it * (HPG * n)
                dve.wait_ge(csb_in[r % 2], 16 * ((HPG * g + r) // 2 + 1) + it * (8 * HPG * n))
                if HPG * g + r >= 2:
                    dve.wait_ge(y_done, h - 1)
                d = eb[:, r % 2, 0:S]
                col = cs_tok[:, :, h:h + 1] if isinstance(h, int) else cs_tok[:, :, bass.ds(h, 1)]
                step(TT(d.rearrange("p (i l) -> p i l", i=NT), csb[:, r % 2, 0:S].rearrange("p (i l) -> p i l", i=NT),
                        col.broadcast_to([P, NT, P]), ALU.subtract))
                TS(d, d, 0.0, None, ALU.min).then_inc(seg_done, 1)

            def decayed(gi, r):
                dve.wait_ge(exp_done, gi * HPG + r + 1)
                if r == 0:
                    dve.wait_ge(cbm_act, gi * 2 + 2)
                TT(eb[:, r % 2, :], eb[:, r % 2, :], cbm[:], ALU.mult).then_inc(m_done, 1)

            def m_body(G, it, n, g, before, proj=True):
                gi, p = g + it * n, g % 2
                for s in range(GSTEP):
                    if s == 0 and before:
                        epilogue(g - 1, 1, 1 - p, it, n)
                        group_sum(gi - 1)
                    if s == 1:
                        if before:
                            group_norm(gi - 1)
                        scaled_x(gi)
                        segment(g, 0, it, n)
                    if s == 2:
                        dve.wait_ge(cb_done, gi + 1)
                        step(TT(cbm[:, 0:S].rearrange("p (i l) -> p i l", i=NT), psum[4][:].rearrange("p (i l) -> p i l", i=NT),
                                tri.unsqueeze(1).broadcast_to([P, NT, P]), ALU.mult))
                    if s >= 2:
                        decayed(gi, s - 2)
                    if 2 <= s <= 4:
                        segment(g, s - 1, it, n)
                    if s == 4:
                        epilogue(g, 0, p, it, n)
                    if proj and s < 4:
                        conv(G, s, it, n)

            for s in range(4):
                conv(0, s, 0, 0)
            dve.wait_ge(tokT_done, 1)
            by_token = lambda bank: bank[:, 0:P].rearrange("p (i h) -> p i h", i=NT)
            nc.vector.tensor_copy(cs_tok[:], by_token(psum[4])).then_inc(tok_ready, 1)
            TS(ncs_tok[:], by_token(psum[4]), -1.0, None, ALU.mult).then_inc(tok_ready, 1)
            nc.vector.tensor_copy(dt_tok[:], by_token(psum[5])).then_inc(tok_ready, 1)
            dve.wait_ge(tok_ready, 3)
            m_body(1, 0, 0, 0, False)
            with dve.Fori(0, 3) as it:
                step.loop(it, 36)
                for b in range(2):
                    m_body(2 + b, it, 2, 1 + b, True)
                step.end(3)
            m_body(8, 0, 0, 7, True, proj=False)
            epilogue(7, 1, 1, 0, 0)
            group_sum(7)
            group_norm(7)
            for k in range(16):
                lo_part(g_lo[:, k, :], y32[:, k, :], g_hi[:, k, :], I0["m_out"] + k)
            clear_acc()
            with dve.Fori(0, 2) as it:
                for m in range(4):
                    add_square(5, m, it, 4)
            residual(2, 6)
            norm_in(3, 6, "f_in1")
            ffn(1)
            norm_in(4, 8, "w_in")

            dve.wait_ge(kc_in, 16 * 8)
            for kv, pos in enumerate(("pos_k", "pos_v")):
                if kv:
                    dve.wait_ge(blk_ready, kv)
                windows = kc2[:, kv].rearrange("p g (c j t) -> p j g c t", j=8, t=2)
                for half in range(2):
                    cols = vec[:, V0[pos] + 8 * half:V0[pos] + 8 * half + 8].unsqueeze(2).broadcast_to([P, 8, NCMP])
                    for e in range(2):
                        ins = TT(blk[:, 8 * half:8 * half + 8, e, :], windows[:, :, e, half:half + NCMP, 0], cols, ALU.add)
                ins.then_inc(blk_out, 1)
                dve.wait_ge(blk_split, kv + 1)
                TT(blk_lo[:], blk[:], blk_hi[:].bitcast(F32), ALU.subtract).then_inc(blk_ready, 1)

            dve.wait_ge(sink_in, 16)
            dve.wait_ge(v_out, 4)
            with dve.Fori(0, 4) as r:
                U = len(UNITS)
                step.loop(r, 98)

                def by_tile(u):
                    return prob_buf(u)[:, 0:P].rearrange("p (i c) -> p i c", i=NT)[:, :, 0:NCMP]

                def score(u):
                    kind, e, qt = UNITS[u]
                    dve.wait_ge(score_done, r * U + u + 1)
                    if u % HALF == 0:
                        dve.wait_ge(bias_in[e], 32 * r + 32)
                    if u >= 4:
                        dve.wait_ge(tr_done, r * U + u - 3)
                    bank = score_bank(u)
                    if kind == "C":
                        for i in range(NT):
                            at = 3 * P + CMP - 1 - i * P
                            ins = STT(out=prob_buf(u)[:, i * 32:i * 32 + NCMP], in0=bank[:, i * 32:i * 32 + NCMP], scalar=0.125,
                                      in1=tbias[:, e, at:at + (NCMP - 1) * STRIDE + 1:STRIDE], op0=ALU.mult, op1=ALU.add)
                    else:
                        k0, k1 = span(kind, qt)
                        w = k1 - k0
                        bias = abias[:, e, TA - w:TA] if kind == "A" else tbias[:, e, S - w:S]
                        ins = STT(out=prob_buf(u)[:, 0:w], in0=bank[:, 0:w], scalar=0.125, in1=bias, op0=ALU.mult, op1=ALU.add)
                    return step.note(ins)

                def maximum(u, scored):
                    kind, e, qt = UNITS[u]
                    n = NT if kind == "C" else 1
                    step.wait(scored)
                    src = by_tile(u) if kind == "C" else prob_buf(u)[:, 0:span(kind, qt)[1] - span(kind, qt)[0]]
                    return step.note(nc.vector.tensor_reduce(stat[:, u % 4, 0, 0:n], src, AX.X, ALU.max))

                def negated(u, most):
                    kind, e, qt = UNITS[u]
                    st, n = stat[:, u % 4], NT if kind == "C" else 1
                    step.wait(most)
                    if kind == "A":
                        step(TT(st[:, 0, 0:1], st[:, 0, 0:1], sinkb[:, bass.ds(r + 4 * e, 1)], ALU.max))
                    TS(st[:, 1, 0:n], st[:, 0, 0:n], -1.0, None, ALU.mult).then_inc(soft_done, 1)

                def total(u):
                    kind, e, qt = UNITS[u]
                    dve.wait_ge(pexp_done, r * U + u + 1)
                    st, n = stat[:, u % 4], NT if kind == "C" else 1
                    if kind == "A":
                        step(TT(st[:, 2, 0:1], st[:, 2, 0:1], st[:, 3, 0:1], ALU.add))
                    return step.note(nc.vector.reciprocal(st[:, 4, 0:n], st[:, 2, 0:n]))

                def normalised(u, inverse):
                    kind, e, qt = UNITS[u]
                    st = stat[:, u % 4]
                    step.wait(inverse)
                    if kind == "C":
                        gate = gates[:, :, bass.ds(r * 3 + 12 * e, 1)].rearrange("p i a -> p (i a)")
                        step(TT(st[:, 4, :], st[:, 4, :], gate, ALU.mult))
                        step(TT(st[:, 4, :], st[:, 4, :], qvalid, ALU.mult))
                        TT(by_tile(u), by_tile(u), st[:, 4, :].unsqueeze(2).broadcast_to([P, NT, NCMP]), ALU.mult).then_inc(pn_done, 1)
                        return
                    k0, k1 = span(kind, qt)
                    p = prob_buf(u)[:, 0:k1 - k0]
                    if kind == "A":
                        TS(p, p, st[:, 4, 0:1], None, ALU.mult).then_inc(pn_done, 1)
                    else:
                        gate = gates[:, qt, bass.ds(r * 3 + (12 * e + 1 + "SW".index(kind)), 1)]
                        TS(p, p, st[:, 4, 0:1], gate, ALU.mult, ALU.mult).then_inc(pn_done, 1)

                for u in range(U + 2):
                    if u < U:
                        scored = score(u)
                    if u >= 2:
                        inverse = total(u - 2)
                    if u < U:
                        most = maximum(u, scored)
                    if u >= 2:
                        normalised(u - 2, inverse)
                    if u < U:
                        negated(u, most)
                for i in range(2):
                    lo_part(tile(h_lo, r + 4 * i), ta[:, i, :], tile(h_hi, r + 4 * i), r * 2 + (I0["up"] + i))
                dve.wait_ge(in_ready, r * 2 + (I0["up"] + 2))
                step.end(4)
            dve.wait_ge(bias_in[0], 32 * 5)

            for u in range(8):
                done(C0["up"] + u)
                for i, buf in enumerate((ta, tb)):
                    t = T0["up"] + 2 * u + i
                    TT(buf[:, u % 2, :], psum[t % 4][:], ga[:, 8 * i + u, :], ALU.mult).then_inc(bank_free[t % 4], 1)
                dve.wait_ge(bank_free[t % 4], t // 4 + 1)
                TT(ta[:, u % 2, :], ta[:, u % 2, :], tb[:, u % 2, :], ALU.add).then_inc(prod_out, 1)
                lo_part(mg_lo[:, u, :], ta[:, u % 2, :], mg_hi[:, u, :], I0["w_out"] + u)
            clear_acc()
            with dve.Fori(0, 2) as it:
                for u in range(4):
                    b = (T0["w_out"] + u) % 4
                    done(C0["w_out"] + u, it, 4)
                    TT(tile(x, it * 4 + u), tile(x, it * 4 + u), psum[b][:], ALU.add).then_inc(bank_free[b], 1)
                    add_square(9, u, it, 4)
            norm_in(5, 9, "g_in")

            with dve.Fori(0, 11) as it:
                step.loop(it, 8)
                for j in range(2):
                    for i, buf in enumerate((ta, tb)):
                        t = T0["g_in"] + 2 * j + i
                        done(C0["g_in"] + 2 * j + i, it, 4)
                        taps(buf[:, j, :], psum[t % 4][:], "g_conv", it * 2 + (KF * i + j), 3, bank_free[t % 4])
                    dve.wait_ge(gate_out, it * 2 + (j + 1))
                    STT(out=ta[:, j, :], in0=ta[:, j, :], scalar=V("g_conv_b", it * 2 + j), in1=sq[:, j, :],
                        op0=ALU.add, op1=ALU.mult).then_inc(prod_out, 1)
                    lo_part(tile(g_lo, it * 2 + j), ta[:, j, :], tile(g_hi, it * 2 + j), it * 2 + (I0["g_out"] + j))
                step.end(11)
            clear_acc()
            for m in range(8):
                b = (T0["g_out"] + m) % 4
                done(C0["g_out"] + 4 * m + 3)
                TT(x[:, m, :], x[:, m, :], psum[b][:], ALU.add).then_inc(bank_free[b], 1)
                add_square(10, m)

            reciprocal(10)
            for k in range(KD):
                if k >= 2:
                    dve.wait_ge(out_done, 16 * (k - 1))
                STT(out=ta[:, k % 2, :], in0=x[:, k, :], scalar=V("norm_final", k), in1=rstd[:],
                    op0=ALU.mult, op1=ALU.mult).then_inc(out_ready, 1)


def bucket(dist):
    exact = BUCKETS // 2
    d = np.maximum(dist, 1).astype(np.float32)
    large = exact + (np.log(d / np.float32(exact)) / np.float32(np.log(128 / exact)) * np.float32(BUCKETS - exact)).astype(np.int32)
    return np.where(dist < exact, np.maximum(dist, 0), np.minimum(large, BUCKETS - 1))


def one_hot(dist, valid):
    rows = np.where(valid, bucket(dist), BUCKETS)
    return (np.arange(BUCKETS + 1)[:, None] == rows[None, :]).astype(np.float32)


def columns(v):
    return np.asarray(v).reshape(-1, P).T


def stationary(w):
    k, m = w.shape
    return w.reshape(k // P, P, m // P, P).transpose(2, 1, 0, 3).reshape(m // P, P, k)


def moving(w):
    k, n = w.shape
    return w.reshape(k // P, P, n).transpose(1, 0, 2).reshape(P, -1)


def halves(t):
    m = t.shape[0]
    return t.reshape(m, P, 2, KF // 2 * P).transpose(0, 2, 1, 3).reshape(2 * m, P, KF // 2 * P)


def interleave(*ts):
    return np.stack(ts, axis=1).reshape((-1,) + ts[0].shape[1:])


def taps_columns(w):
    width, n = w.shape
    return w.reshape(width, n // P, P).transpose(2, 1, 0).reshape(P, -1)


def by_group(t, n):
    x, b, c = t[:2 * GROUPS].reshape(GROUPS, 2, *t.shape[1:]), t[2 * GROUPS:3 * GROUPS][:, None], t[3 * GROUPS:4 * GROUPS][:, None]
    parts = [x, b, c]
    if n == 6:
        parts.append(t[4 * GROUPS:].reshape(GROUPS, 2, *t.shape[1:]))
    return np.concatenate(parts, axis=1).reshape(t.shape)


def head_pairs(n_first):
    return np.concatenate([np.arange(h * 64, h * 64 + 64) for r in range(4) for h in (r, r + 4)]) + n_first


def layout(a):
    ins = {}
    vecs = dict(c=columns(a["c"]), ada_b=columns(a["ada_b"]), norm_g=columns(a["norm_g"]),
                a_conv=taps_columns(a["a_conv_w"][0]),
                m_norm=columns(a["m_norm_g"]), m_d=columns(np.repeat(a["m_d"][0], 64)),
                pos_k=a["cmp_pos_k_2"][0].reshape(16, P).T, pos_v=a["cmp_pos_v_2"][0].reshape(16, P).T,
                norm_mix=columns(a["norm_mix_2"]), norm_ffn=columns(a["norm_ffn_2"]), norm_final=columns(a["norm_final_2"]),
                g_conv=taps_columns(a["conv_w_2"][0]), g_conv_b=columns(a["conv_b_2"]))
    conv = a["m_conv_w"][0].reshape(4, 4 * GROUPS, P).transpose(1, 2, 0)
    vecs["m_conv"] = by_group(conv, 4).transpose(1, 0, 2).reshape(P, -1)
    vecs["m_conv_b"] = by_group(a["m_conv_b"][0].reshape(4 * GROUPS, P), 4).T
    ins["vec"] = np.concatenate([vecs[n] for n in VCOLS], axis=1)
    qvalid = np.ones((P, NT))
    qvalid[:CMP - 1, 0] = 0
    ins["kst"] = np.concatenate([np.eye(P), np.triu(np.ones((P, P))), qvalid], axis=1).astype(np.float32)
    ins["dtp"] = np.stack([a["m_dt_bias"][0], a["m_a_log"][0]], axis=1)
    ins["x"] = moving(a["x"][0].T)
    ada = a["ada_w"]
    ins["ada"] = ada.reshape(KD, P, 48, 256).transpose(2, 1, 0, 3).reshape(48, P, KD * 256)
    b, c, v = (stationary(w) for w in np.split(a["a_w_in"][0], 3, axis=1))
    ins["a_in"] = interleave(c, v, b)
    ins["a_out"] = stationary(a["a_w_out"][0])
    for i in range(2):
        ins[f"f_in{i}"] = interleave(*(stationary(w) for w in np.split(a["f_w_in"][i], 2, axis=1)))
        ins[f"f_out{i}"] = halves(stationary(a["f_w_out"][i]))
    m = a["m_w_in"][0]
    z, xbc, dt = m[:, :16 * P], m[:, 16 * P:48 * P], m[:, 48 * P:]
    dt = np.concatenate([dt, np.zeros((D, P - HEADS), np.float32)], axis=1)
    mo = stationary(a["m_w_out"][0])
    ins["m"] = np.concatenate([stationary(dt), by_group(np.concatenate([stationary(xbc), stationary(z)]), 6),
                               mo.reshape(8, P, 2, D).transpose(0, 2, 1, 3).reshape(16, P, D)])
    w = a["w_in_2"][0]
    at = dict(zip("qa ka va qb kc vc ks vs kw vw gn ga gb".split(),
                  np.cumsum([0, 512, 128, 128, 512, 128, 128, 128, 128, 128, 128, 24, 1024])))
    part = lambda n, width=P: w[:, at[n]:at[n] + width]
    gn = np.concatenate([part("gn", 24), np.zeros((D, P - 24), np.float32)], axis=1)
    ins["w_in"] = stationary(np.concatenate([w[:, head_pairs(at["qa"])], w[:, head_pairs(at["qb"])]]
                                            + [part(n) for n in "ka ks kw kc vc va vs vw".split()]
                                            + [gn, part("ga", D), part("gb", D)], axis=1))
    cmp = np.concatenate([stationary(a[n][0]).reshape(2, P, 2, D).transpose(0, 2, 1, 3).reshape(4, P, D)
                                 for n in ("cmp_w1_k_2", "cmp_w1_v_2")])
    order = {w_chunk(u): t for u, t in enumerate(ins["w_in"])} | {cmp_chunk(i): t for i, t in enumerate(cmp)}
    ins["w_in"] = np.stack([order[c] for c in range(CHUNKS["w_in"])])
    ins["w2"] = np.stack([a[n][0].reshape(2, P, 64).transpose(1, 0, 2) for n in ("cmp_w2_k_2", "cmp_w2_v_2")])
    up = np.concatenate([a[n][0][head_pairs(0)] for n in ("w_up_a_2", "w_up_b_2")])
    ins["up"] = stationary(up)
    ins["w_out"] = stationary(a["w_out_2"][0])
    ins["g_in"] = interleave(*(stationary(w) for w in np.split(a["w_ffn_in_2"][0], 2, axis=1)))
    ins["g_out"] = halves(stationary(a["w_ffn_out_2"][0]))
    ins["tbl"] = np.concatenate([a["rel_bias_table_2"], np.full((1, 16), NEG, np.float32)])
    db, da = S - 1 - np.arange(WB), 2 * P - 1 - np.arange(WA)
    ins["hot"] = np.concatenate([one_hot(db, db >= 0), one_hot(da, (da >= 0) & (da < P))], axis=1)
    ins["sinks"] = a["attn_sinks_2"]
    return {n: np.ascontiguousarray(v) for n, v in ins.items()}


def kernel(**arrays):
    import concourse.bacc as bacc
    from concourse.bass_utils import run_bass_kernel_spmd
    ins = layout({n: np.asarray(v) for n, v in arrays.items()})
    nc = bacc.Bacc("TRN2", target_bir_lowering=False, num_devices=1)
    io = {n: nc.dram_tensor(n + "_d", v.shape, F32, kind="ExternalInput").ap() for n, v in ins.items()}
    io["out"] = nc.dram_tensor("out_d", [KD, P, S], F32, kind="ExternalOutput").ap()
    io["cs"] = nc.dram_tensor("cs_d", [HEADS, PACK], F32, kind="Internal").ap()
    io["brow"] = nc.dram_tensor("brow_d", [16, WB + WA], F32, kind="Internal").ap()
    io["rows"] = nc.dram_tensor("rows_d", [16, P * (WB + 1)], F32, kind="Internal").ap()
    program(nc, io)
    result = run_bass_kernel_spmd(nc, [{n + "_d": v for n, v in ins.items()}], core_ids=[0])
    out = result.results[0]["out_d"]
    return np.ascontiguousarray(out.reshape(D, S).T)[None]
```
